# Optimizing a Trainium2 kernel written in Bass

```python
import math
import jax, jax.numpy as jnp
from jax import lax
import numpy as np

D_MODEL = 1024
BATCH = 1
SEQ = 1024
DEPTH = 2

N_A = DEPTH // 2
N_B = DEPTH - N_A
CONV_WIDTH = 31
CONV_CH = D_MODEL
N_HEADS = 8
QK_NOPE_DIM = 128
QK_ROPE_DIM = 64
V_HEAD_DIM = 128
Q_LORA_RANK = 384
KV_LORA_RANK = 256
ROPE_THETA = 10000.0
Q_BLOCK = 128
ATTN_SCALE = 1.0 / math.sqrt(QK_NOPE_DIM + QK_ROPE_DIM)
N_EXPERTS = 16
N_GROUPS = 4
EXPERTS_PER_GROUP = N_EXPERTS // N_GROUPS
TOP_K = 2
D_EXPERT = 512
ROW_BLOCK = 128
EPS = 1e-6
NEG_INF = -1e30

kernel_name = "yoco_conformer_mla_grouped_moe_adaln"

def rms_norm(x, g):
    xf = x.astype(jnp.float32)
    y = xf * lax.rsqrt(jnp.mean(xf * xf, axis=-1, keepdims=True) + EPS)
    return (y * g.astype(jnp.float32)).astype(x.dtype)

def layer_norm(x, g, b):
    xf = x.astype(jnp.float32)
    mu = jnp.mean(xf, axis=-1, keepdims=True)
    var = jnp.mean(jnp.square(xf - mu), axis=-1, keepdims=True)
    y = (xf - mu) * lax.rsqrt(var + EPS)
    return (y * g.astype(jnp.float32) + b.astype(jnp.float32)).astype(x.dtype)

def modulate(x, g, shift, scale):
    return rms_norm(x, g) * (1 + scale[:, None, :]) + shift[:, None, :]

def rope_tables(positions, dtype):
    inv_freq = ROPE_THETA ** (-jnp.arange(0, QK_ROPE_DIM, 2, dtype=jnp.float32) / QK_ROPE_DIM)
    ang = positions.astype(jnp.float32)[..., None] * inv_freq
    return jnp.cos(ang).astype(dtype), jnp.sin(ang).astype(dtype)

def apply_rope(x, cos, sin):
    x1, x2 = jnp.split(x, 2, axis=-1)
    return jnp.concatenate([x1 * cos - x2 * sin, x1 * sin + x2 * cos], axis=-1)

def conformer_conv(h, w_in, b_in, w_dw, b_dw, ln_g, ln_b, w_out):
    u = h @ w_in + b_in
    a, gate = jnp.split(u, 2, axis=-1)
    u = a * jax.nn.sigmoid(gate)
    u = lax.conv_general_dilated(
        u, w_dw[:, None, :], window_strides=(1,), padding=[(CONV_WIDTH - 1, 0)],
        dimension_numbers=("NWC", "WIO", "NWC"), feature_group_count=CONV_CH) + b_dw
    u = jax.nn.silu(layer_norm(u, ln_g, ln_b))
    return u @ w_out

def shared_kv(x, kv_in_g, w_dkv, kv_norm_g, w_ukv, cos, sin):
    Bsz, S, _ = x.shape
    ckv = rms_norm(x, kv_in_g) @ w_dkv
    latent = rms_norm(ckv[..., :KV_LORA_RANK], kv_norm_g)
    k_rope = apply_rope(ckv[..., KV_LORA_RANK:], cos, sin)
    kv = (latent @ w_ukv).reshape(Bsz, S, N_HEADS, QK_NOPE_DIM + V_HEAD_DIM)
    return kv[..., :QK_NOPE_DIM], k_rope, kv[..., QK_NOPE_DIM:]

def mla_attention(q_nope, q_rope, k_nope, k_rope, v):
    Bsz, S, H, _ = q_nope.shape
    nb = S // Q_BLOCK
    qn = q_nope.reshape(Bsz, nb, Q_BLOCK, H, QK_NOPE_DIM).transpose(1, 0, 2, 3, 4)
    qr = q_rope.reshape(Bsz, nb, Q_BLOCK, H, QK_ROPE_DIM).transpose(1, 0, 2, 3, 4)
    q_pos = jnp.arange(S, dtype=jnp.int32).reshape(nb, Q_BLOCK)
    k_pos = jnp.arange(S, dtype=jnp.int32)

    def one_block(args):
        qn_b, qr_b, qp = args
        s = (jnp.einsum("bqhd,bkhd->bhqk", qn_b, k_nope)
             + jnp.einsum("bqhr,bkr->bhqk", qr_b, k_rope)).astype(jnp.float32) * ATTN_SCALE
        s = jnp.where(k_pos[None, :] <= qp[:, None], s, NEG_INF)
        p = jax.nn.softmax(s, axis=-1).astype(v.dtype)
        return jnp.einsum("bhqk,bkhd->bqhd", p, v)

    o = lax.map(one_block, (qn, qr, q_pos))
    return o.transpose(1, 0, 2, 3, 4).reshape(Bsz, S, H * V_HEAD_DIM)

def route(h2, router_w, router_b):
    T = h2.shape[0]
    s = jax.nn.sigmoid(h2.astype(jnp.float32) @ router_w.astype(jnp.float32))
    sb = (s + router_b.astype(jnp.float32)).reshape(T, N_GROUPS, EXPERTS_PER_GROUP)
    grp_score = lax.top_k(sb, 2)[0].sum(-1)
    g = jnp.argmax(grp_score, axis=-1).astype(jnp.int32)
    within = jnp.take_along_axis(sb, g[:, None, None], axis=1)[:, 0]
    _, loc = lax.top_k(within, TOP_K)
    idx = g[:, None] * EXPERTS_PER_GROUP + loc.astype(jnp.int32)
    w = jnp.take_along_axis(s, idx, axis=1)
    return idx, w / jnp.sum(w, axis=-1, keepdims=True)

def moe_ffn(h, router_w, router_b, w_gate, w_up, w_down):
    Bsz, S, D = h.shape
    T = Bsz * S
    h2 = h.reshape(T, D)
    idx, w = route(h2, router_w, router_b)
    flat_e = idx.reshape(-1)
    flat_w = w.reshape(-1).astype(h.dtype)
    flat_tok = jnp.repeat(jnp.arange(T, dtype=jnp.int32), TOP_K)
    order = jnp.argsort(flat_e)
    sorted_e = flat_e[order]
    counts = jnp.bincount(flat_e, length=N_EXPERTS)
    padded = ((counts + ROW_BLOCK - 1) // ROW_BLOCK) * ROW_BLOCK
    pad_end = jnp.cumsum(padded)
    pad_start = pad_end - padded
    start = jnp.cumsum(counts) - counts
    rank = jnp.arange(T * TOP_K, dtype=jnp.int32) - start[sorted_e]
    dest = pad_start[sorted_e] + rank
    n_rows = T * TOP_K + N_EXPERTS * ROW_BLOCK
    n_blk = n_rows // ROW_BLOCK
    buf_tok = jnp.full((n_rows,), T, jnp.int32).at[dest].set(flat_tok[order])
    buf_w = jnp.zeros((n_rows,), h.dtype).at[dest].set(flat_w[order])
    blk_start = jnp.arange(n_blk, dtype=pad_end.dtype) * ROW_BLOCK
    blk_e = jnp.minimum(jnp.searchsorted(pad_end, blk_start, side="right"), N_EXPERTS - 1)
    h_pad = jnp.concatenate([h2, jnp.zeros((1, D), h.dtype)], axis=0)
    xb = h_pad[buf_tok].reshape(n_blk, ROW_BLOCK, D)

    def expert_block(args):
        xr, e = args
        return (jax.nn.silu(xr @ w_gate[e]) * (xr @ w_up[e])) @ w_down[e]

    yb = lax.map(expert_block, (xb, blk_e)).reshape(n_rows, D)
    y = jnp.zeros((T + 1, D), h.dtype).at[buf_tok].add(yb * buf_w[:, None])[:T]
    return y.reshape(Bsz, S, D)

def setup_inputs(seed: int = 0) -> dict:
    key = jax.random.key(seed)
    ks = iter(jax.random.split(key, 40))
    D = D_MODEL
    f32 = jnp.float32

    def nrm(shape, scale):
        return jax.random.normal(next(ks), shape, f32) * scale

    def gain(shape):
        return 1.0 + 0.05 * jax.random.normal(next(ks), shape, f32)

    x = jax.random.normal(next(ks), (BATCH, SEQ, D), f32)
    c = jax.random.normal(next(ks), (BATCH, D), f32)
    offs = jax.random.randint(next(ks), (BATCH, 1), 0, 1024, dtype=jnp.int32)
    positions = offs + jnp.arange(SEQ, dtype=jnp.int32)[None, :]
    return {
        "x": x, "c": c, "positions": positions,
        "ada_w": nrm((DEPTH, D, 6 * D), 0.5 * D ** -0.5),
        "ada_b": nrm((DEPTH, 6 * D), 0.02),
        "norm1_g": gain((DEPTH, D)),
        "norm2_g": gain((DEPTH, D)),
        "conv_w_in": nrm((N_A, D, 2 * CONV_CH), D ** -0.5),
        "conv_b_in": nrm((N_A, 2 * CONV_CH), 0.02),
        "conv_w_dw": nrm((N_A, CONV_WIDTH, CONV_CH), CONV_WIDTH ** -0.5),
        "conv_b_dw": nrm((N_A, CONV_CH), 0.02),
        "conv_ln_g": gain((N_A, CONV_CH)),
        "conv_ln_b": nrm((N_A, CONV_CH), 0.02),
        "conv_w_out": nrm((N_A, CONV_CH, D), CONV_CH ** -0.5),
        "kv_in_g": gain((D,)),
        "w_dkv": nrm((D, KV_LORA_RANK + QK_ROPE_DIM), D ** -0.5),
        "kv_norm_g": gain((KV_LORA_RANK,)),
        "w_ukv": nrm((KV_LORA_RANK, N_HEADS * (QK_NOPE_DIM + V_HEAD_DIM)), KV_LORA_RANK ** -0.5),
        "w_dq": nrm((N_B, D, Q_LORA_RANK), D ** -0.5),
        "q_norm_g": gain((N_B, Q_LORA_RANK)),
        "w_uq": nrm((N_B, Q_LORA_RANK, N_HEADS * (QK_NOPE_DIM + QK_ROPE_DIM)), Q_LORA_RANK ** -0.5),
        "w_o": nrm((N_B, N_HEADS * V_HEAD_DIM, D), (N_HEADS * V_HEAD_DIM) ** -0.5),
        "router_w": nrm((D, N_EXPERTS), D ** -0.5),
        "router_b": nrm((N_EXPERTS,), 0.01),
        "exp_w_gate": nrm((DEPTH, N_EXPERTS, D, D_EXPERT), D ** -0.5),
        "exp_w_up": nrm((DEPTH, N_EXPERTS, D, D_EXPERT), D ** -0.5),
        "exp_w_down": nrm((DEPTH, N_EXPERTS, D_EXPERT, D), D_EXPERT ** -0.5),
        "final_g": gain((D,)),
    }

def reference(x, c, positions, ada_w, ada_b, norm1_g, norm2_g,
              conv_w_in, conv_b_in, conv_w_dw, conv_b_dw, conv_ln_g, conv_ln_b, conv_w_out,
              kv_in_g, w_dkv, kv_norm_g, w_ukv,
              w_dq, q_norm_g, w_uq, w_o,
              router_w, router_b, exp_w_gate, exp_w_up, exp_w_down, final_g):
    Bsz, S, _ = x.shape
    cos, sin = rope_tables(positions, x.dtype)
    c_act = jax.nn.silu(c)
    k_nope = k_rope = v = None
    for l in range(DEPTH):
        mod = c_act @ ada_w[l] + ada_b[l]
        sh1, sc1, g1, sh2, sc2, g2 = jnp.split(mod, 6, axis=-1)
        h = modulate(x, norm1_g[l], sh1, sc1)
        if l < N_A:
            mix = conformer_conv(h, conv_w_in[l], conv_b_in[l], conv_w_dw[l], conv_b_dw[l],
                                 conv_ln_g[l], conv_ln_b[l], conv_w_out[l])
        else:
            j = l - N_A
            if j == 0:
                k_nope, k_rope, v = shared_kv(x, kv_in_g, w_dkv, kv_norm_g, w_ukv, cos, sin)
            cq = rms_norm(h @ w_dq[j], q_norm_g[j])
            q = (cq @ w_uq[j]).reshape(Bsz, S, N_HEADS, QK_NOPE_DIM + QK_ROPE_DIM)
            q_nope = q[..., :QK_NOPE_DIM]
            q_rope = apply_rope(q[..., QK_NOPE_DIM:], cos[:, :, None, :], sin[:, :, None, :])
            mix = mla_attention(q_nope, q_rope, k_nope, k_rope, v) @ w_o[j]
        x = x + g1[:, None, :] * mix
        h = modulate(x, norm2_g[l], sh2, sc2)
        x = x + g2[:, None, :] * moe_ffn(h, router_w, router_b,
                                         exp_w_gate[l], exp_w_up[l], exp_w_down[l])
    return rms_norm(x, final_g)


_drawn_inputs = setup_inputs


def setup_inputs(seed=0):
    import zlib

    import numpy as np

    out = dict(_drawn_inputs(seed))
    spreads = {}
    factors = {'conv_b_in': 4.428,
     'conv_b_dw': 3.038,
     'conv_ln_b': 2.982,
     'kv_in_g': 5.385,
     'kv_norm_g': 6.268,
     'q_norm_g': 7.008}
    for name, (base, spread) in spreads.items():
        noise = np.random.default_rng([zlib.crc32(name.encode()), seed]).standard_normal(out[name].shape)
        drawn = base * np.exp(spread * noise) if base else spread * noise
        out[name] = __import__('jax').numpy.asarray(drawn.astype(out[name].dtype))
    for name, factor in factors.items():
        out[name] = (out[name] * factor).astype(out[name].dtype)
    return out
```

```python
from contextlib import ExitStack

import concourse.bass as bass
import numpy as np
from concourse import mybir

F32 = mybir.dt.float32
F32R = mybir.dt.float32r
I32 = mybir.dt.int32
ALU = mybir.AluOpType
ACT = mybir.ActivationFunctionType
AX_X = mybir.AxisListType.X

P = 128
D = 1024
S = 1024
KD = D // P
NT = S // P
HALF = 512
TAPS = 31
PAD = TAPS - 1
NH = 8
NOPE = 128
ROPE = 64
QR = 384
KVR = 256
NE = 16
NG = 4
EPG = NE // NG
DE = 512
EPS = 1e-6
NEG = -1e30
ATTN_SCALE = 1.0 / float(np.sqrt(NOPE + ROPE))
MAX_BLOCKS = 2 * S // P + NE
ROW_BLOCKS = MAX_BLOCKS + 2

VEC_ROWS = [("c", 8), ("norm1_g", 16), ("norm2_g", 16), ("kv_in_g", 8), ("conv_b_in", 16), ("conv_b_dw", 8),
            ("conv_ln_g", 8), ("conv_ln_b", 8), ("kv_norm_g", 2), ("q_norm_g", 3)]
COL = {}
_at = 0
for _name, _n in VEC_ROWS:
    COL[_name] = _at
    _at += _n
NVEC = _at
COL_ADA_B = 96
COL_DW = 192
DW_ROWS = TAPS * KD // 2
COL_POS = COL_DW + 2 * DW_ROWS
NCOL = COL_POS + NT
ADA_Q = 4
ADA_CHUNKS = 2 * 6 * ADA_Q
ADA_FIRST = 2 * ADA_Q
ADA_PER_C = (ADA_CHUNKS - ADA_FIRST) // KD
ADA_SLOTS = 5
TWO_PI = 2 * np.pi
C1 = 6.28125
C2 = float(np.float32(np.float16(TWO_PI - C1)))
C3 = float(TWO_PI - C1 - C2)
ROUND = 1.5 * 2.0 ** 23


def build_trunk(nc, a, out):
    sorted_rows = nc.dram_tensor("sorted_rows", (ROW_BLOCKS * P, D), F32, kind="Internal").ap()
    x_res = [nc.dram_tensor(f"x_res{l}", (S, D), F32, kind="Internal").ap() for l in range(2)]
    x_mid = nc.dram_tensor("x_mid", (S, D), F32, kind="Internal").ap()

    with ExitStack() as ctx:
        def sb(name, *shape, dt=F32):
            return ctx.enter_context(nc.sbuf_tensor(name, [P, *shape], dt))

        def sem(name):
            return ctx.enter_context(nc.semaphore(name))

        def sems(name, n):
            return [sem(f"{name}{i}") for i in range(n)]

        ident = sb("ident", P)
        before = sb("before", P)
        ones = sb("ones", P)
        causal = sb("causal", P)
        cols = sb("cols", NCOL)
        modc = sb("modc", 96)
        gainc = sb("gainc", 4, KD)
        gate_row = sb("gate_row", 2, D)
        scratch = sb("scratch", D)
        cosr = sb("cosr", NT, ROPE // 2)
        sinr = sb("sinr", NT, ROPE // 2)
        invf = sb("invf", ROPE // 2)
        c_col = sb("c_col", KD)
        ssq = sb("ssq", NT)
        rstd = sb("rstd", NT)
        mv = sb("mv", NT, 2)
        bst = sb("bst", 2 * NT, 6)
        neghalf = sb("neghalf", NT)
        router = sb("router", KD, NE)
        router_bias = sb("router_bias", NE)
        rt = sb("rt", 12, P)
        rcol = sb("rcol", 8, NT)
        w_lo = sb("w_lo", NT)
        w_hi = sb("w_hi", NT)
        d_lo = sb("d_lo", NT, dt=I32)
        d_hi = sb("d_hi", NT, dt=I32)
        starts = sb("starts", NE + 1, dt=I32)
        sm = sb("sm", 48)
        g_lo = sb("g_lo", NT, dt=I32)
        g_hi = sb("g_hi", NT, dt=I32)
        ps = ctx.enter_context(nc.psum_tensor("ps", [P, 8, HALF], F32))

        base = -(-nc.sbuf_base // 64) * 64
        X_SIZE = NT * D
        room = (nc.sbuf_usable_end - base) // 4 - X_SIZE

        def at(name, offset, *shape, dt=F32):
            assert offset + int(np.prod(shape)) <= room, (name, offset, shape, room)
            return nc.alloc_sbuf_tensor_at(name, [P, *shape], dt, offset=base + 4 * (offset + X_SIZE))

        xr = at("xr", -X_SIZE, NT, D)
        vec_rows = at("vec_rows", 0, 4, P)
        pos_rows = at("pos_rows", 4 * P, P, dt=I32)
        pos_rows_f = at("pos_rows_f", 5 * P, P)
        hT = at("hT", 0, KD, S)
        w_in = [at(f"w_in{u}", 8192 + 2048 * u, KD, 2, P) for u in range(2)]
        ada_w = [at(f"ada_w{s}", 12288 + 2048 * s, KD, 2, P) for s in range(ADA_SLOTS)]
        w_out = at("w_out", 4096, KD, D)
        glu = at("glu", 22528, PAD + S)
        sig = at("sig", 23584, 2, HALF)
        acc = [at(f"acc{u}", 24640 + S * u, S) for u in range(2)]
        vT = [at(f"vT{u}", 26688 + D * u, KD, P) for u in range(2)]
        v_tok = at("v_tok", 28800, NT, D)
        mix_t = at("mix_t", 24640, D)
        zero = at("zero", 37000, HALF)
        angle = [at(f"angle{n}", 24640 + 256 * n, NT, ROPE // 2) for n in range(4)]
        raw = [at(f"raw_{n}", 4096 * n - X_SIZE, 4, 1024) for n in range(3)]
        part_h = [at(f"w{n}_h", 4096 + 8192 * n, 4, 1024, dt=F32R) for n in range(3)]
        part_l = [at(f"w{n}_l", 8192 + 8192 * n, 4, 1024, dt=F32R) for n in range(3)]
        h_rows = at("h_rows", 12288, NT, D)
        mod_row = at("mod_row", 22528, 2, D)
        h2T = [at(f"h2T{u}", 20480 + D * u, KD, P) for u in range(2)]
        rows = at("rows", 28672, D)
        rowsT_h = at("rowsT_h", 29696, KD, P, dt=F32R)
        rowsT_l = at("rowsT_l", 30720, KD, P, dt=F32R)
        act = at("act", 31744, DE)
        hid = at("hid", 32256, DE)
        hidT_h = at("hidT_h", 32768, DE // P, P, dt=F32R)
        hidT_l = at("hidT_l", 33280, DE // P, P, dt=F32R)
        y_sb = at("y_sb", 33792, D)
        got = [at(f"got{n}", 21504 + D * n, D)[:] for n in range(3)] + [rt[:, 0:8, :].rearrange("p a b -> p (a b)")]
        fin = [at(f"fin{n}", 8192 + D * n, D) for n in range(2)]
        final_row = at("final_row", 10240, D)
        xn_t = [at(f"xn_t{u}", 8192 + D * u, D) for u in range(2)]
        xnT = [at(f"xnT{u}", 10240 + D * u, KD, P) for u in range(2)]
        qinT = [at(f"qinT{u}", 12288 + D * u, KD, P) for u in range(2)]
        lat = [at(f"lat{u}", 14336 + 384 * u, 3, P) for u in range(2)]
        cqn = [at(f"cqn{u}", 15104 + 384 * u, 3, P) for u in range(2)]
        qro = [at(f"qro{u}", 15872 + 512 * u, NH, ROPE) for u in range(2)]
        rope_t = at("rope_t", 16896, 4, NH, ROPE // 2)
        w_dq = at("w_dq", 18432, KD, QR)
        w_ukv = at("w_ukv", 0, KVR // P, NH, 2, P)
        w_dkv = at("w_dkv", 4096, KD, KVR + ROPE)
        w_uqr = at("w_uqr", 6656, QR // P, NH, ROPE)
        latT = at("latT", 24576, KVR // P, S)
        cqT = at("cqT", 26624, QR // P, S)
        w_uqn = at("w_uqn", 29696, QR // P, NH, P)
        kT = at("kT", 16384, NH, S)
        v_all = at("v_all", 8192, NT, NH, P)
        qT = at("qT", 0, NH, S)
        w_o = at("w_o", 24576, NH, D)
        krT = at("krT", 32768, S)
        qrT = at("qrT", 33792, NH // 2, S)
        mix_t2 = at("mix_t2", 33792, D)
        xflat = xr[:].rearrange("p a b -> p (a b)")
        probs = [xflat[:, S * u:S * (u + 1)] for u in range(2)]
        probsT = [xflat[:, 2048 + S * u:2048 + S * (u + 1)].rearrange("p (a b) -> p a b", b=P) for u in range(2)]

        consts_ok, vec_in, vec_T, vec_ok, c_ok = sem("consts_ok"), sem("vec_in"), sem("vec_T"), sem("vec_ok"), sem("c_ok")
        x_in = sems("x_in", 2)
        misc_in, zero_ok, zeroed = sem("misc_in"), sem("zero_ok"), sem("zeroed")
        ada_in, ada_used = sems("ada_in", ADA_SLOTS), sem("ada_used")
        mod_first, mod_ok = sem("mod_first"), sem("mod_ok")
        win_in, wout_in = sems("win_in", 2), sem("wout_in")
        pool_own, dve_own = sem("pool_own"), sem("dve_own")
        ssq_ok, rstd_ok, xn_ok = sem("ssq_ok"), sem("rstd_ok"), sem("xn_ok")
        in_T, hT_ok = sem("in_T"), sem("hT_ok")
        uv_ready, sig_ok, uv_free, tap_done = sem("uv_ready"), sem("sig_ok"), sem("uv_free"), sem("tap_done")
        conv_T, conv_ev = sem("conv_T"), sem("conv_ev")
        ln_ok, ln_rstd, vn_ok, vn_T, vT_ok, mix_ok, mixed = (sem("ln_ok"), sem("ln_rstd"), sem("vn_ok"), sem("vn_T"), sem("vT_ok"),
                                                             sem("mix_ok"), sem("mixed"))
        diag_ok, row_ps, row_ok = sem("diag_ok"), sem("row_ps"), sem("row_ok")
        ang_ok, trig_ok = sem("ang_ok"), sem("trig_ok")

        PIECES = 4
        weights_in, weights_hi, weights_lo = sems("w_in_", 3), sems("w_hi_", 3), sems("w_lo_", 3)
        x_back = sem("x_back")
        rows_got = sems("rows_got", 4)

        class Layer:

            def __init__(self, l):
                def s(n):
                    return sem(f"{n}_l{l}")
                self.l = l
                self.xn, self.T, self.h2T, self.logit = s("m_h"), s("m_T"), s("m_h2T"), s("m_logit")
                self.score, self.mask, self.rank, self.plan = s("m_score"), s("m_mask"), s("m_rank"), s("m_plan")
                self.scattered = s("m_scattered")
                self.w_in, self.hi, self.lo = weights_in, weights_hi, weights_lo
                self.n_in, self.n_split = l * 16 * NE, l * PIECES * NE
                self.n_down = self.n_split + l * PIECES
                self.rows_in, self.rows_T, self.rowsT_h, self.rowsT_l = s("m_rows_in"), s("m_rows_T"), s("m_rowsT_h"), s("m_rowsT_l")
                self.gate, self.up, self.silu = s("m_gate"), s("m_up"), s("m_silu")
                self.hid, self.hid_T, self.hidT_h, self.hidT_l, self.down = s("m_hid"), s("m_hid_T"), s("m_hidT_h"), s("m_hidT_l"), s("m_down")
                self.y, self.y_out, self.all_out = s("m_y"), s("m_y_out"), s("m_all_out")
                self.got, self.got_base = rows_got, l * 16 * NT // 2
                self.x, self.saved = s("m_x"), s("m_saved")

        layers = [Layer(0), Layer(1)]
        mid_out, mid_in, out_done = sem("mid_out"), sems("mid_in", 2), sems("out_done", 2)
        aw_in = sems("aw_in", 6)
        folded = sem("folded")
        a_xn, a_T1, a_xnT, a_M, a_ss, a_r, a_nrm, a_T2, a_ev2, a_R, a_qr, a_T3, a_ev3 = (
            sem(f"a_{n}") for n in ("xn", "T1", "xnT", "M", "ss", "r", "nrm", "T2", "ev2", "R", "qr", "T3", "ev3"))
        k_ps, k_ev, v_ps, v_ev, q_ps, q_ev = (sem(n) for n in ("k_ps", "k_ev", "v_ps", "v_ev", "q_ps", "q_ev"))
        s_ok, nb_ok, p_ok, pT_ps, pT_a, pT_v, o_ps, o_ok, o_T, oT_a, oT_v, m_ps, m_ev = (
            sem(n) for n in ("s_ok", "nb_ok", "p_ok", "pT_ps", "pT_a", "pT_v", "o_ps", "o_ok", "o_T", "oT_a", "oT_v", "m_ps", "m_ev"))
        f_ok = sem("f_ok")

        UNITS = [(i, h) for i in range(NT) for h in range(NH)]
        WO_ORDER = [4, 5, 6, 7, 0, 1, 2, 3]
        TILE_ORDER = [list(range(NT)), WO_ORDER]

        def col(name, k, n=1):
            return cols[:, COL[name] + k:COL[name] + k + n]

        def mod(l, comp, k, n=1):
            at0 = l * 48 + comp * 8 + k
            return modc[:, at0:at0 + n]

        def banks(b):
            return ps[:, b:b + 2, :].rearrange("p b c -> p (b c)")

        def ada_src(g):
            l, q = divmod(g, 6 * ADA_Q)
            return a["ada_w"][l].rearrange("(k p) n -> p k n", p=P)[:, :, q * 256:(q + 1) * 256].rearrange(
                "p k (t n) -> p k t n", n=P)

        w_in_src = a["conv_w_in"][0].rearrange("(k p) (g c n) -> c p k g n", p=P, g=2, n=P)
        block = ctx.enter_context(nc.Block())

        @block.sync
        def _(sp):
            for name, n in VEC_ROWS:
                src = a[name]
                if len(src.shape) == 2:
                    src = src.rearrange("a b -> (a b)")
                sp.dma_start(vec_rows[COL[name]:COL[name] + n, 0, :], src.rearrange("(r n) -> r n", n=P)).then_inc(vec_in, 16)
            sp.dma_start(vec_rows[0:96, 1, :], a["ada_b"].rearrange("l (r n) -> (l r) n", n=P)).then_inc(vec_in, 16)
            dw = a["conv_w_dw"][0].rearrange("t (k n) -> (t k) n", n=P)
            for u in range(2):
                sp.dma_start(vec_rows[0:DW_ROWS, 2 + u, :], dw[u * DW_ROWS:(u + 1) * DW_ROWS, :]).then_inc(vec_in, 16)
            sp.dma_start(pos_rows[0:NT, :], a["positions"].rearrange("a (r n) -> (a r) n", n=P)).then_inc(vec_in, 16)
            xsrc = a["x"][0].rearrange("(t p) d -> t p d", p=P)
            for i in range(NT):
                sp.dma_start(xr[:, i, :], xsrc[i]).then_inc(x_in[i // 4], 16)

            def load_ada(g):
                if g >= ADA_SLOTS:
                    sp.wait_ge(ada_used, g - ADA_SLOTS + 1)
                sp.dma_start(ada_w[g % ADA_SLOTS][:], ada_src(g)).then_inc(ada_in[g % ADA_SLOTS], 16)

            for g in range(ADA_FIRST):
                load_ada(g)
            sp.dma_start(invf[:], a["inv_freq"].partition_broadcast(P)).then_inc(misc_in, 16)
            sp.dma_start(router[:], a["router_w"].rearrange("(k p) e -> p k e", p=P)).then_inc(misc_in, 16)
            sp.dma_start(router_bias[:], a["router_b"].partition_broadcast(P)).then_inc(misc_in, 16)

            def load_w_in(c):
                if c >= 2:
                    sp.wait_ge(uv_ready, 2 * (c - 1))
                for g in range(2):
                    sp.dma_start(w_in[c % 2][:, :, g, :], w_in_src[c][:, :, g, :]).then_inc(win_in[c % 2], 16)

            load_w_in(0)
            load_w_in(1)
            for c in range(KD):
                for g in range(ADA_FIRST + ADA_PER_C * c, ADA_FIRST + ADA_PER_C * (c + 1)):
                    load_ada(g)
                if c + 2 < KD:
                    load_w_in(c + 2)
            sp.wait_ge(uv_ready, 2 * KD)
            sp.dma_start(w_out[:], a["conv_w_out"][0].rearrange("(k p) d -> p k d", p=P)).then_inc(wout_in, 16)

            WEIGHTS = ("exp_w_gate", "exp_w_up", "exp_w_down")

            def load_matrix(m, n, e):
                nk = (KD, KD, DE // P)[n]
                src = a[WEIGHTS[n]][m.l].rearrange("e (k p) n -> p (e k) n", p=P)[:, bass.ds(e * nk, nk), :]
                dst = raw[n][:] if n == 2 else raw[n][:].rearrange("p c (k n) -> p (c k) n", n=DE)
                sp.dma_start(dst, src).then_inc(m.w_in[n], 16)

            def load_first(m):
                for n, i in enumerate(TILE_ORDER[m.l]):
                    sp.wait_ge((mixed, m_ev)[m.l], 2 * n + 2)
                    sp.dma_start(x_res[m.l][i * P:(i + 1) * P, :], xr[:, i, :]).then_inc(m.saved, 16)
                sp.wait_ge(m.saved, 16 * NT)
                sp.wait_ge(m.xn, NT)
                sp.wait_ge(ssq_ok, (2 + 2 * m.l) * NT)
                for n in range(3):
                    if n == 2 and m.l:
                        sp.wait_ge(m_ps, 2 * NT)
                    load_matrix(m, n, 0)

            def load_experts(m):
                with sp.Fori(1, NE) as e:
                    for n in range(3):
                        before_n = m.n_down + PIECES if n == 2 else m.n_split
                        sp.wait_ge(m.lo[n], e * PIECES + before_n)
                        load_matrix(m, n, e)
                for n in range(3):
                    sp.wait_ge(m.lo[n], (m.n_down + PIECES if n == 2 else m.n_split) + PIECES * NE)
                for i in range(NT):
                    sp.dma_start(xr[:, i, :], x_res[m.l][i * P:(i + 1) * P, :]).then_inc(x_back, 16)

            m = layers[0]
            load_first(m)
            load_experts(m)
            sp.wait_ge(m.all_out, 1)
            sp.dma_start(w_dkv[:], a["w_dkv"].rearrange("(k p) n -> p k n", p=P)).then_inc(aw_in[0], 16)
            sp.dma_start(w_dq[:], a["w_dq"][0].rearrange("(k p) n -> p k n", p=P)).then_inc(aw_in[1], 16)
            uq = a["w_uq"][0].rearrange("(k p) (h n) -> p k h n", p=P, h=NH)
            for k in range(QR // P):
                sp.dma_start(w_uqr[:, k], uq[:, k, :, NOPE:]).then_inc(aw_in[2], 16)
                sp.dma_start(w_uqn[:, k], uq[:, k, :, 0:NOPE]).then_inc(aw_in[3], 16)
            sp.dma_start(w_ukv[:].rearrange("p k h t n -> p k (h t n)"), a["w_ukv"].rearrange("(k p) n -> p k n", p=P)).then_inc(aw_in[4], 16)
            for i in range(NT):
                sp.wait_ge(m.x, i + 1)
                sp.dma_start(x_mid[i * P:(i + 1) * P, :], xr[:, i, :]).then_inc(mid_out, 16)
            sp.wait_ge(q_ps, 2 * NH)
            sp.dma_start(w_o[:], a["w_o"][0].rearrange("(h p) n -> p h n", p=P)).then_inc(aw_in[5], 16)
            m = layers[1]
            sp.wait_ge(mid_out, 16 * NT)
            sp.wait_ge(a_xn, NT)
            for n, i in enumerate(WO_ORDER):
                if n == 4:
                    sp.wait_ge(o_ps, len(UNITS))
                sp.dma_start(xr[:, i, :], x_mid[i * P:(i + 1) * P, :]).then_inc(mid_in[n // 4], 16)
            load_first(m)
            load_experts(m)
            sp.wait_ge(m.all_out, 1)
            sp.dma_start(final_row[:], a["final_g"].partition_broadcast(P)).then_inc(misc_in, 16)
            dst = out[0].rearrange("(t p) d -> t p d", p=P)
            for i in range(NT):
                sp.wait_ge(f_ok, i + 1)
                sp.dma_start(dst[i], fin[i % 2][:]).then_inc(out_done[i % 2], 16)
            for u in range(2):
                sp.wait_ge(out_done[u], 16 * NT // 2)

        @block.gpsimd
        def _(pool):
            own = Count(pool, pool_own)
            for t, v in ((ident, 0.0), (before, 1.0), (ones, 1.0), (causal, 0.0), (neghalf, -0.5)):
                own.chain(nc.gpsimd.memset(t[:], v))
            nc.gpsimd.affine_select(out=ident[:], in_=ident[:], compare_op=ALU.not_equal, fill=1.0, base=0,
                                    pattern=[[-1, P]], channel_multiplier=1).then_inc(consts_ok, 1)
            nc.gpsimd.affine_select(out=before[:], in_=before[:], compare_op=ALU.is_gt, fill=0.0, base=0,
                                    pattern=[[1, P]], channel_multiplier=-1).then_inc(consts_ok, 1)
            nc.gpsimd.affine_select(out=causal[:], in_=causal[:], compare_op=ALU.is_ge, fill=NEG, base=0,
                                    pattern=[[-1, P]], channel_multiplier=1).then_inc(consts_ok, 1)
            nc.gpsimd.memset(zero[:], 0.0).then_inc(zero_ok, 1)

            def root(dst, src, scale, done):
                own.chain(nc.gpsimd.tensor_scalar(dst, src, scale, EPS, ALU.mult, ALU.add))
                nc.gpsimd.tensor_tensor(dst, dst, neghalf[:, 0:dst.shape[1]], ALU.pow).then_inc(done, 1)

            pool.wait_ge(ssq_ok, NT)
            root(rstd[:], ssq[:], 1.0 / D, rstd_ok)
            pool.wait_ge(zero_ok, 1)
            pool.wait_ge(hT_ok, 2 * KD)
            pool.dma_start(sorted_rows.rearrange("a b -> (a b)").rearrange("(p r n) -> p r n", p=P, n=HALF),
                           zero[:].unsqueeze(1).to_broadcast([P, 2 * ROW_BLOCKS, HALF])).then_inc(zeroed, 16)
            pool.wait_ge(ln_ok, NT)
            root(rstd[:], mv[:, :, 1], 1.0, ln_rstd)

            def roots(m):
                for n, i in enumerate(TILE_ORDER[m.l]):
                    pool.wait_ge(ssq_ok, (1 + 2 * m.l) * NT + n + 1)
                    root(rstd[:, i:i + 1], ssq[:, i:i + 1], 1.0 / D, rstd_ok)

            def scatter(m):
                pool.wait_ge(m.plan, 1)
                pool.wait_ge(zeroed, 16)
                for i in range(NT):
                    for d in (d_lo, d_hi):
                        pool.indirect_dma_start(sorted_rows, bass.IndirectOffsetOnAxis(ap=d[:, i:i + 1], axis=0), h_rows[:, i, :],
                                                None).then_inc(m.scattered, 16)
                pool.wait_ge(m.all_out, 1)

            def gather(m, i):
                for n, d in enumerate((g_lo, g_hi)):
                    buf = 2 * (i % 2) + n
                    if i >= 2:
                        pool.wait_ge(m.x, i - 1)
                    pool.indirect_dma_start(got[buf], None, sorted_rows, bass.IndirectOffsetOnAxis(ap=d[:, i:i + 1], axis=0)
                                            ).then_inc(m.got[buf], 16)

            def last_roots(base, i):
                pool.wait_ge(ssq_ok, base + i + 1)
                root(rstd[:, i:i + 1], ssq[:, i:i + 1], 1.0 / D, rstd_ok)

            roots(layers[0])
            scatter(layers[0])
            def q_roots(i):
                pool.wait_ge(a_ss, i + 1)
                own.chain(nc.gpsimd.tensor_scalar(sm[:, 16:17], sm[:, 0:1], 1.0 / KVR, EPS, ALU.mult, ALU.add))
                own.chain(nc.gpsimd.tensor_scalar(sm[:, 17:18], sm[:, 1:2], 1.0 / QR, EPS, ALU.mult, ALU.add))
                nc.gpsimd.tensor_tensor(sm[:, 18:20], sm[:, 16:18], neghalf[:, 0:2], ALU.pow).then_inc(a_r, 1)

            for i in range(NT + 3):
                if i < NT:
                    gather(layers[0], i)
                if 1 <= i <= NT:
                    last_roots(2 * NT, i - 1)
                if i >= 3:
                    q_roots(i - 3)
            roots(layers[1])
            scatter(layers[1])
            for i in range(NT + 1):
                if i < NT:
                    gather(layers[1], i)
                if i:
                    last_roots(4 * NT, i - 1)

        @block.scalar
        def _(act_e):
            act_e.wait_ge(vec_ok, 1)
            nc.scalar.activation(c_col[:], col("c", 0, KD), ACT.Silu).then_inc(c_ok, 1)

            squared = Count(act_e, ssq_ok)

            def squares(i):
                if squared.n:
                    act_e.wait_ge(ssq_ok, squared.n)
                squared.n += 1
                nc.scalar.activation(scratch[:], xr[:, i, :], ACT.Square, accum_out=ssq[:, i:i + 1]).then_inc(ssq_ok, 1)

            for i in range(NT):
                act_e.wait_ge(x_in[i // 4], 64)
                squares(i)
            for n in range(2 * KD):
                g, k = divmod(n, KD)
                act_e.wait_ge(in_T, n + 1)
                act_e.wait_ge(mod_first, 1)
                nc.scalar.activation(hT[:, k, g * HALF:(g + 1) * HALF], ps[:, n % 4, :], ACT.Identity, bias=mod(0, 0, k),
                                     scale=gainc[:, 0, k:k + 1]).then_inc(hT_ok, 1)
            act_e.wait_ge(ang_ok, 1)
            nc.scalar.activation(cosr[:], angle[1][:], ACT.Sin).then_inc(trig_ok, 1)
            nc.scalar.activation(sinr[:], angle[0][:], ACT.Sin).then_inc(trig_ok, 1)

            def gates(c):
                act_e.wait_ge(uv_ready, 2 * c + 2)
                for half in range(2):
                    nc.scalar.activation(sig[:, half, :], ps[:, 2 * half + 1, :], ACT.Sigmoid,
                                         bias=cols[:, bass.ds(c + (COL["conv_b_in"] + KD), 1)]).then_inc(sig_ok, 1)

            def conv_out(c):
                for half in range(2):
                    act_e.wait_ge(conv_T, 2 * c + half + 1)
                    nc.scalar.activation(v_tok[:, 4 * half:4 * half + 4, bass.ds(c * P, P)],
                                         ps[:, 4 + half, :].rearrange("p (t n) -> p t n", n=P), ACT.Copy).then_inc(conv_ev, 1)

            gates(0)
            with act_e.Fori(0, KD // 2 - 1) as j:
                for u in range(2):
                    gates(2 * j + (u + 1))
                    conv_out(2 * j + u)
            gates(KD - 1)
            conv_out(KD - 2)
            conv_out(KD - 1)

            def gate_rows(l, rs):
                for r in rs:
                    act_e.wait_ge(row_ps, 4 * l + r + 1)
                    dst = gate_row if r < 2 else mod_row
                    nc.scalar.activation(dst[:, r % 2, :], banks(4 + 2 * (r % 2)), ACT.Copy).then_inc(row_ok, 1)

            gate_rows(0, range(4))

            def route(m, n):
                i = TILE_ORDER[m.l]
                if 1 <= n <= NT:
                    act_e.wait_ge((mixed, m_ev)[m.l], 2 * n)
                    squares(i[n - 1])
                if 2 <= n <= NT + 1:
                    act_e.wait_ge(m.T, n - 1)
                    if n >= 4:
                        act_e.wait_ge(m.logit, n - 3)
                    nc.scalar.activation(h2T[n % 2][:].rearrange("p k n -> p (k n)"), banks(2), ACT.Copy).then_inc(m.h2T, 1)

            for n in range(-1, NT + 2):
                if 0 <= n + 1 < NT:
                    act_e.wait_ge(vn_T, n + 2)
                    if n >= 1:
                        act_e.wait_ge(mix_ok, 2 * n)
                    for k in range(KD):
                        nc.scalar.activation(vT[(n + 1) % 2][:, k, :], banks(0)[:, k * P:(k + 1) * P], ACT.Silu,
                                             bias=col("conv_ln_b", k), scale=col("conv_ln_g", k)).then_inc(vT_ok, 1)
                route(layers[0], n)

            def moe(m):
                act_e.wait_ge(m.logit, NT)
                nc.scalar.activation(rt[:, 0, :], ps[:, 6, 0:P], ACT.Sigmoid).then_inc(m.score, 1)

                def split_hi(n, n_in):
                    act_e.wait_ge(m.w_in[n], n_in)
                    for c in range(PIECES):
                        nc.scalar.activation(part_h[n][:, c, :], raw[n][:, c, :], ACT.Copy).then_inc(m.hi[n], 1)

                def load_rows(b):
                    act_e.dma_start(rows[:], sorted_rows[bass.ds(b * P, P), :]).then_inc(m.rows_in, 16)

                def rowsT():
                    nc.scalar.activation(rowsT_h[:].rearrange("p k n -> p (k n)"), banks(2), ACT.Copy).then_inc(m.rowsT_h, 1)

                def hidT():
                    nc.scalar.activation(hidT_h[:].rearrange("p k n -> p (k n)"), ps[:, 4, :], ACT.Copy).then_inc(m.hidT_h, 1)

                act_e.wait_ge(m.plan, 1)
                split_hi(0, m.n_in + 16)
                act_e.wait_ge(m.scattered, 16 * 2 * NT)
                load_rows(0)
                split_hi(1, m.n_in + 16)
                act_e.wait_ge(m.rows_T, 1)
                rowsT()
                load_rows(1)
                split_hi(2, m.n_in + 16)

                def expert(e, has_next):
                    first = act_e.value_load(starts[0:1, bass.ds(e, 1)], min_val=0, max_val=MAX_BLOCKS)
                    end = act_e.value_load(starts[0:1, bass.ds(e + 1, 1)], min_val=1, max_val=MAX_BLOCKS)
                    with act_e.Fori(first, end) as b:
                        act_e.wait_ge(m.gate, b + 1)
                        nc.scalar.activation(act[:], ps[:, 0, :], ACT.Silu).then_inc(m.silu, 1)
                        act_e.wait_ge(m.hid_T, b + 1)
                        hidT()
                        if has_next:
                            with act_e.If(b + 1 == end):
                                split_hi(0, e * 16 + (m.n_in + 32))
                        act_e.wait_ge(m.rows_T, b + 2)
                        rowsT()
                        load_rows(b + 2)
                        if has_next:
                            with act_e.If(b + 1 == end):
                                split_hi(1, e * 16 + (m.n_in + 32))
                        act_e.wait_ge(m.y, b + 2)
                        act_e.dma_start(sorted_rows[bass.ds(b * P, P), :], y_sb[:]).then_inc(m.y_out, 16)
                        with act_e.If(b == first):
                            act_e.wait_ge(m.down, b + 1)
                            split_hi(2, e * 16 + (m.n_in + 16))

                with act_e.Fori(0, NE - 1) as e:
                    expert(e, True)
                expert(NE - 1, False)
                total = act_e.value_load(starts[0:1, NE:NE + 1], min_val=NE, max_val=MAX_BLOCKS)
                act_e.wait_ge(m.hid_T, total + 1)
                hidT()
                act_e.wait_ge(m.y, total + 2)
                act_e.dma_start(sorted_rows[bass.ds(total * P, P), :], y_sb[:]).then_inc(m.y_out, 16)
                act_e.wait_ge(m.y_out, 16 * total + 32)
                act_e.wait_ge(m.rows_in, 16 * total + 32)
                nc.scalar.activation(sm[:, 40:41], sm[:, 40:41], ACT.Copy).then_inc(m.all_out, 1)

            def last_squares(m, i):
                act_e.wait_ge(m.x, i + 1)
                squares(i)

            moe(layers[0])
            gate_rows(1, range(2))

            def fold(name, k, dst):
                nc.scalar.activation(dst, dst, ACT.Copy, scale=col(name, k)).then_inc(folded, 1)

            def copy_xnT(i):
                act_e.wait_ge(a_T1, i + 1)
                if i >= 2:
                    act_e.wait_ge(a_M, i - 1)
                nc.scalar.activation(xnT[i % 2][:].rearrange("p k n -> p (k n)"), banks(0), ACT.Copy)
                for k in range(KD):
                    last = nc.scalar.activation(qinT[i % 2][:, k, :], banks(0)[:, k * P:(k + 1) * P], ACT.Identity, bias=mod(1, 0, k),
                                                scale=gainc[:, 2, k:k + 1])
                last.then_inc(a_xnT, 1)

            def latent_squares(i):
                act_e.wait_ge(a_M, i + 1)
                if i >= 1:
                    act_e.wait_ge(a_nrm, i)
                act_e.wait_ge(ssq_ok, squared.n)
                nc.scalar.activation(scratch[:, 0:KVR], ps[:, 2, 0:KVR], ACT.Square, accum_out=sm[:, 0:1])
                nc.scalar.activation(scratch[:, KVR:KVR + QR], ps[:, 3, 0:QR], ACT.Square, accum_out=sm[:, 1:2]).then_inc(a_ss, 1)

            def copy_latT(i):
                act_e.wait_ge(a_T2, i + 1)
                tok = slice(i * P, (i + 1) * P)
                nc.scalar.activation(latT[:, :, tok], ps[:, 4, 0:KVR].rearrange("p (k n) -> p k n", n=P), ACT.Copy).then_inc(a_ev2, 1)
                nc.scalar.activation(krT[:, tok], ps[:, 4, KVR:KVR + P], ACT.Copy).then_inc(a_ev2, 1)
                nc.scalar.activation(cqT[:, :, tok], ps[:, 5, 0:QR].rearrange("p (k n) -> p k n", n=P), ACT.Copy).then_inc(a_ev2, 1)

            def copy_qrT(i):
                act_e.wait_ge(a_T3, i + 1)
                nc.scalar.activation(qrT[:, :, i * P:(i + 1) * P], ps[:, 7, :].rearrange("p (k n) -> p k n", n=P),
                                     ACT.Copy).then_inc(a_ev3, 1)

            act_e.wait_ge(aw_in[0], 16)
            for k in range(KD):
                fold("kv_in_g", k, w_dkv[:, k, :])
            act_e.wait_ge(aw_in[2], 48)
            for k in range(QR // P):
                fold("q_norm_g", k, w_uqr[:, k].rearrange("p h n -> p (h n)"))
            last_squares(layers[0], 0)
            last_squares(layers[0], 1)
            copy_xnT(0)
            for i in range(NT + 2):
                if i + 2 < NT:
                    if i >= 1:
                        act_e.wait_ge(a_ss, i)
                    last_squares(layers[0], i + 2)
                if i + 1 < NT:
                    copy_xnT(i + 1)
                if i < NT:
                    latent_squares(i)
                if 1 <= i <= NT:
                    copy_latT(i - 1)
                if i >= 2:
                    copy_qrT(i - 2)
            act_e.wait_ge(aw_in[4], 16)
            for k in range(KVR // P):
                fold("kv_norm_g", k, w_ukv[:, k].rearrange("p h t n -> p (h t n)"))
            act_e.wait_ge(aw_in[3], 48)
            for k in range(QR // P):
                fold("q_norm_g", k, w_uqn[:, k].rearrange("p h n -> p (h n)"))
            for n in range(2 * NH):
                act_e.wait_ge(k_ps, n + 1)
                h, half = divmod(n, 2)
                nc.scalar.activation(kT[:, h, half * HALF:(half + 1) * HALF], ps[:, n % 2, :], ACT.Copy).then_inc(k_ev, 1)
            for n in range(2 * NH):
                act_e.wait_ge(q_ps, n + 1)
                h, half = divmod(n, 2)
                nc.scalar.activation(qT[:, h, half * HALF:(half + 1) * HALF], ps[:, 4 + n % 2, :], ACT.Copy).then_inc(q_ev, 1)
            act_e.wait_ge(mid_out, 16 * NT)
            for u, (i, h) in enumerate(UNITS):
                n = (i + 1) * P
                act_e.wait_ge(nb_ok, u + 1)
                nc.scalar.activation(probs[u % 2][:, 0:n], banks(2 * (u % 2))[:, 0:n], ACT.Exp, bias=sm[:, 4 + u % 4:5 + u % 4],
                                     scale=ATTN_SCALE, accum_out=sm[:, 8 + u % 4:9 + u % 4]).then_inc(p_ok, 1)
                act_e.wait_ge(pT_ps, u + 1)
                n = min(n, HALF)
                nc.scalar.activation(probsT[u % 2][:, 0:n // P, :], ps[:, 4, 0:n].rearrange("p (k n) -> p k n", n=P),
                                     ACT.Copy).then_inc(pT_a, 1)
                if h == 1 and i > 0 or u == len(UNITS) - 1:
                    j = i - 1 if u < len(UNITS) - 1 else i
                    act_e.wait_ge(o_T, j + 1)
                    nc.scalar.activation(qT[:, 0:4, j * P:(j + 1) * P], ps[:, 6, :].rearrange("p (k n) -> p k n", n=P),
                                         ACT.Copy).then_inc(oT_a, 1)
            gate_rows(1, range(2, 4))
            for n in range(NT + 2):
                route(layers[1], n)
            moe(layers[1])
            for i in range(NT):
                last_squares(layers[1], i)

        @block.vector
        def _(dve):
            own = Count(dve, dve_own)
            ch = own.chain
            V = nc.vector

            dve.wait_ge(vec_in, 16 * (len(VEC_ROWS) + 4))
            ch(V.tensor_copy(pos_rows_f[0:NT, :], pos_rows[0:NT, :]))
            V.memset(glu[:, 0:PAD], 0.0).then_inc(uv_free, 2)
            V.memset(sm[:, 43:44], 0.0).then_inc(conv_ev, 2)
            dve.wait_ge(vec_T, 1)
            ch(V.tensor_copy(cols[:, 0:NVEC], ps[:, 7, 0:NVEC]))
            V.tensor_copy(cols[:, COL_ADA_B:NCOL], ps[:, 7, COL_ADA_B:NCOL]).then_inc(vec_ok, 1)
            dve.wait_ge(vec_ok, 1)

            def normalise(dst, i):
                return V.tensor_scalar(dst, xr[:, i, :], rstd[:, i:i + 1], None, ALU.mult)

            dve.wait_ge(rstd_ok, 1)
            for i in range(NT):
                normalise(v_tok[:, i, :], i).then_inc(xn_ok, 1)
            dve.wait_ge(ada_used, ADA_FIRST)
            ch(V.tensor_tensor(modc[:, 0:16], ps[:, 6, 0:16], cols[:, COL_ADA_B:COL_ADA_B + 16], ALU.add))
            V.scalar_tensor_tensor(gainc[:, 0, :], mod(0, 1, 0, KD), 1.0, col("norm1_g", 0, KD), ALU.add, ALU.mult).then_inc(mod_first, 1)
            dve.wait_ge(misc_in, 48)
            for i in range(NT):
                ch(V.tensor_scalar(angle[0][:, i, :], invf[:], cols[:, COL_POS + i:COL_POS + i + 1], None, ALU.mult))
            ch(V.tensor_scalar(angle[1][:], angle[0][:], 1.0 / TWO_PI, ROUND, ALU.mult, ALU.add))
            ch(V.tensor_scalar(angle[1][:], angle[1][:], ROUND, None, ALU.subtract))
            for part in (C1, C2, C3):
                ch(V.scalar_tensor_tensor(angle[0][:], angle[1][:], -part, angle[0][:], ALU.mult, ALU.add))
            PI = float(np.nextafter(np.float32(np.pi), np.float32(0)))
            ch(V.tensor_scalar(angle[0][:], angle[0][:], PI, -PI, ALU.min, ALU.max))
            ch(V.tensor_scalar(angle[2][:], angle[0][:], -1.0, None, ALU.mult))
            ch(V.tensor_tensor(angle[1][:], angle[0][:], angle[2][:], ALU.max))
            V.tensor_scalar(angle[1][:], angle[1][:], -1.0, float(np.pi / 2), ALU.mult, ALU.add).then_inc(ang_ok, 1)

            PER_C = 2 * TAPS + 2

            def taps(c, u):
                n = 0
                for half in range(2):
                    dve.wait_ge(sig_ok, 2 * c + half + 1)
                    V.scalar_tensor_tensor(glu[:, PAD + half * HALF:PAD + (half + 1) * HALF], ps[:, 2 * half, :],
                                           cols[:, bass.ds(c + COL["conv_b_in"], 1)], sig[:, half, :], ALU.add,
                                           ALU.mult).then_inc(uv_free, 1)
                dve.wait_ge(uv_free, 2 * c + 4)
                for t in range(TAPS):
                    w = cols[:, bass.ds(c + (COL_DW + t * KD), 1)]
                    for half in range(2):
                        src = glu[:, t + half * HALF:t + half * HALF + HALF]
                        dst = acc[u][:, half * HALF:(half + 1) * HALF]
                        if t == 0:
                            V.tensor_scalar(dst, src, w, cols[:, bass.ds(c + COL["conv_b_dw"], 1)], ALU.mult, ALU.add).then_inc(tap_done, 1)
                        else:
                            dve.wait_ge(tap_done, 2 * TAPS * c + (2 * t + half - 1))
                            V.scalar_tensor_tensor(dst, src, w, dst, ALU.mult, ALU.add).then_inc(tap_done, 1)
                dve.wait_ge(tap_done, 2 * TAPS * c + 2 * TAPS)

            with dve.Fori(0, KD // 2) as j:
                for u in range(2):
                    taps(2 * j + u, u)

            dve.wait_ge(ada_used, ADA_CHUNKS)
            ch(V.tensor_tensor(modc[:, 16:96], ps[:, 7, 0:80], cols[:, COL_ADA_B + 16:COL_ADA_B + 96], ALU.add))
            for l in range(2):
                for r, name in enumerate(("norm1_g", "norm2_g")):
                    if l or r:
                        ch(V.scalar_tensor_tensor(gainc[:, 2 * l + r, :], mod(l, 1 + 3 * r, 0, KD), 1.0, col(name, KD * l, KD), ALU.add, ALU.mult))
            V.memset(sm[:], 0.0).then_inc(mod_ok, 1)

            def gate_rows(l, rs):
                for r in rs:
                    if l or r:
                        dve.wait_ge(row_ps, 4 * l + r)
                    for k in range(KD):
                        c = gainc[:, 2 * l + 1, k:k + 1] if r == 2 else mod(l, (2, 5, 4, 3)[r], k)
                        V.tensor_scalar(scratch[:, k * P:(k + 1) * P], ident[:], c, None, ALU.mult).then_inc(diag_ok, 1)

            dve.wait_ge(ssq_ok, NT)
            gate_rows(0, range(4))
            for i in range(NT):
                dve.wait_ge(conv_ev, 2 * KD + 2)
                for half in range(2):
                    V.bn_stats(bst[:, 2 * i + half, :], v_tok[:, i, half * HALF:(half + 1) * HALF]).then_inc(dve_own, 1)
                    own.n += 1
            dve.wait_ge(dve_own, own.n)
            for i in range(NT):
                V.bn_aggr(mv[:, i, :], bst[:, 2 * i:2 * i + 2, :].rearrange("p a b -> p (a b)")).then_inc(ln_ok, 1)
            dve.wait_ge(ln_ok, NT)
            dve.wait_ge(ln_rstd, 1)

            def add_mixed(i, half, temp, ready, n, done):
                sl = slice(half * HALF, (half + 1) * HALF)
                dve.wait_ge(ready, n)
                ch(V.tensor_tensor(temp[:, sl], ps[:, 4 + half, :], gate_row[:, 0, sl], ALU.mult))
                V.tensor_tensor(xr[:, i, sl], xr[:, i, sl], temp[:, sl], ALU.add).then_inc(done, 1)

            def modulated(m, n):
                i = TILE_ORDER[m.l][n]
                dve.wait_ge(rstd_ok, (1, NT + 1 + NT)[m.l] + n + 1)
                ch(V.scalar_tensor_tensor(h_rows[:, i, :], xr[:, i, :], rstd[:, i:i + 1], mod_row[:, 0, :], ALU.mult, ALU.mult))
                V.tensor_tensor(h_rows[:, i, :], h_rows[:, i, :], mod_row[:, 1, :], ALU.add).then_inc(m.xn, 1)

            dve.wait_ge(row_ok, 4)
            for n in range(-1, NT + 1):
                if n + 1 < NT:
                    i = n + 1
                    V.tensor_scalar(v_tok[:, i, :], v_tok[:, i, :], mv[:, i, 0:1], rstd[:, i:i + 1], ALU.subtract, ALU.mult).then_inc(vn_ok, 1)
                if n >= 1:
                    modulated(layers[0], n - 1)
                if 0 <= n < NT:
                    for half in range(2):
                        add_mixed(n, half, mix_t, mix_ok, 2 * n + half + 1, mixed)

            def moe(m):
                l = m.l
                dve.wait_ge(m.score, 1)
                s, sbias, rank, cmp_, mask, sM, work, pre, tot = (rt[:, n, :] for n in range(9))
                G = NT * NG
                per_j = rank.rearrange("p (j g) -> p j g", j=EPG)
                sb_g = sbias.rearrange("p (g j) -> p g j", j=EPG)
                ch(V.tensor_tensor(sbias.rearrange("p (t e) -> p t e", e=NE), s.rearrange("p (t e) -> p t e", e=NE),
                                   router_bias[:].unsqueeze(1).to_broadcast([P, NT, NE]), ALU.add))

                def ranks(n, rank_of, value_of, width):
                    for x in range(n):
                        ch(V.memset(rank_of(x), float(n - 1 - x)))
                    for x in range(n):
                        for y in range(x + 1, n):
                            c = cmp_[:, 0:width]
                            ch(V.tensor_tensor(c, value_of(x), value_of(y), ALU.is_ge))
                            ch(V.tensor_tensor(rank_of(y), rank_of(y), c, ALU.add))
                            ch(V.tensor_tensor(rank_of(x), rank_of(x), c, ALU.subtract))

                ranks(EPG, lambda j: per_j[:, j, :], lambda j: sb_g[:, :, j], G)
                ch(V.tensor_scalar(rank, rank, 1.5, None, ALU.is_lt))
                ch(V.tensor_tensor(work.rearrange("p (g j) -> p g j", j=EPG), sb_g, rank.rearrange("p (j g) -> p g j", j=EPG), ALU.mult))
                gs = rcol[:, 0:4, :].rearrange("p a b -> p (a b)")
                ch(V.tensor_reduce(gs, work.rearrange("p (g j) -> p g j", j=EPG), AX_X, ALU.add))
                gs_t = gs.rearrange("p (t g) -> p t g", g=NG)
                grank = rcol[:, 4:8, :]
                ranks(NG, lambda g: grank[:, g, :], lambda g: gs_t[:, :, g], NT)
                ch(V.tensor_scalar(grank, grank, 0.5, None, ALU.is_lt))
                mask_j = mask.rearrange("p (t g j) -> p t g j", g=NG, j=EPG)
                for j in range(EPG):
                    ch(V.tensor_tensor(mask_j[:, :, :, j], per_j[:, j, :].rearrange("p (t g) -> p t g", g=NG),
                                       grank.rearrange("p g t -> p t g"), ALU.mult))
                V.tensor_tensor(sM, s, mask, ALU.mult).then_inc(m.mask, 1)
                dve.wait_ge(m.mask, 1)

                def by_expert(v):
                    return v.rearrange("p (t e) -> p t e", e=NE)

                def per_tile(v):
                    return v.unsqueeze(2).to_broadcast([P, NT, NE])

                wsum, rw, hi, lo = (rcol[:, n, :] for n in range(4))
                ch(V.tensor_reduce(wsum, by_expert(sM), AX_X, ALU.add))
                ch(V.reciprocal(rw, wsum))
                dve.wait_ge(m.rank, 1)
                ch(V.tensor_copy(pre, ps[:, 7, 0:P]))
                ch(V.tensor_copy(tot, ps[:, 7, P:2 * P]))
                run = sm[:, 0:NE]
                ch(V.memset(run, 0.0))
                for t in range(NT):
                    sl = slice(t * NE, (t + 1) * NE)
                    ch(V.tensor_tensor(pre[:, sl], pre[:, sl], run, ALU.add))
                    ch(V.tensor_tensor(run, run, tot[:, sl], ALU.add))
                nblk, inc = sm[:, NE:2 * NE], [rt[:, 9, 0:NE], rt[:, 10, 0:NE]]
                ch(V.memset(nblk, 1.0))
                for n in range(1, S // P):
                    ch(V.scalar_tensor_tensor(nblk, run, float(P * n), nblk, ALU.is_gt, ALU.add))
                ch(V.tensor_copy(inc[0], nblk))
                cur, step = 0, 1
                while step < NE:
                    ch(V.tensor_copy(inc[1 - cur][:, 0:step], inc[cur][:, 0:step]))
                    ch(V.tensor_tensor(inc[1 - cur][:, step:], inc[cur][:, step:], inc[cur][:, 0:NE - step], ALU.add))
                    cur, step = 1 - cur, 2 * step
                first = rt[:, 11, 0:NE]
                ch(V.tensor_tensor(first, inc[cur], nblk, ALU.subtract))
                ch(V.tensor_copy(starts[:, 0:NE], first))
                ch(V.tensor_copy(starts[:, NE:NE + 1], inc[cur][:, NE - 1:NE]))
                ch(V.tensor_scalar(first, first, float(P), 1.0, ALU.mult, ALU.add))
                ch(V.tensor_tensor(by_expert(pre), by_expert(pre), first.unsqueeze(1).to_broadcast([P, NT, NE]), ALU.add))
                ch(V.tensor_tensor(pre, pre, mask, ALU.mult))
                ch(V.tensor_reduce(hi, by_expert(pre), AX_X, ALU.max))
                ch(V.tensor_reduce(lo, by_expert(pre), AX_X, ALU.add))
                ch(V.tensor_tensor(lo, lo, hi, ALU.subtract))
                for d, w, dest in ((hi, w_hi, d_hi), (lo, w_lo, d_lo)):
                    ch(V.tensor_tensor(by_expert(work), by_expert(pre), per_tile(d), ALU.is_equal))
                    ch(V.tensor_tensor(work, work, sM, ALU.mult))
                    ch(V.tensor_reduce(w[:], by_expert(work), AX_X, ALU.add))
                    ch(V.tensor_tensor(w[:], w[:], rw, ALU.mult))
                    ch(V.tensor_scalar(dest[:], d, -1.0, None, ALU.add))
                    ch(V.tensor_scalar((g_hi if w is w_hi else g_lo)[:], d, float(P - 1), None, ALU.add))
                V.memset(sm[:, 40:41], 0.0).then_inc(m.plan, 1)
                V.memset(sm[:, 44:45], 0.0).then_inc(m.y, 1)
                V.memset(sm[:, 45:46], 0.0).then_inc(m.y_out, 16)
                V.memset(hid[:], 0.0).then_inc(m.hid, 1)

                def split_lo(n, count):
                    for c in range(PIECES):
                        dve.wait_ge(m.hi[n], count + (c + 1))
                        V.tensor_tensor(part_l[n][:, c, :], raw[n][:, c, :], part_h[n][:, c, :].bitcast(F32), ALU.subtract
                                        ).then_inc(m.lo[n], 1)

                def rowsT():
                    V.tensor_tensor(rowsT_l[:].rearrange("p k n -> p (k n)"), banks(2), rowsT_h[:].rearrange("p k n -> p (k n)").bitcast(F32),
                                    ALU.subtract).then_inc(m.rowsT_l, 1)

                def hidT():
                    V.tensor_tensor(hidT_l[:].rearrange("p k n -> p (k n)"), ps[:, 4, :], hidT_h[:].rearrange("p k n -> p (k n)").bitcast(F32),
                                    ALU.subtract).then_inc(m.hidT_l, 1)

                def output():
                    V.tensor_tensor(y_sb[:], banks(5), gate_row[:, 1, :], ALU.mult).then_inc(m.y, 1)

                split_lo(0, m.n_split)
                split_lo(1, m.n_split)
                dve.wait_ge(m.rowsT_h, 1)
                rowsT()
                split_lo(2, m.n_down)

                def expert(e, has_next):
                    first = dve.value_load(starts[0:1, bass.ds(e, 1)], min_val=0, max_val=MAX_BLOCKS)
                    end = dve.value_load(starts[0:1, bass.ds(e + 1, 1)], min_val=1, max_val=MAX_BLOCKS)
                    with dve.Fori(first, end) as b:
                        dve.wait_ge(m.hidT_h, b + 1)
                        hidT()
                        if has_next:
                            with dve.If(b + 1 == end):
                                split_lo(0, e * PIECES + (m.n_split + PIECES))
                        dve.wait_ge(m.silu, b + 1)
                        dve.wait_ge(m.up, b + 1)
                        V.tensor_tensor(hid[:], act[:], ps[:, 1, :], ALU.mult).then_inc(m.hid, 1)
                        dve.wait_ge(m.rowsT_h, b + 2)
                        rowsT()
                        if has_next:
                            with dve.If(b + 1 == end):
                                split_lo(1, e * PIECES + (m.n_split + PIECES))
                        dve.wait_ge(m.down, b + 1)
                        dve.wait_ge(m.y_out, b * 16 + 16)
                        output()
                        with dve.If(b == first):
                            split_lo(2, e * PIECES + (m.n_down + PIECES))

                with dve.Fori(0, NE - 1) as e:
                    expert(e, True)
                expert(NE - 1, False)
                total = dve.value_load(starts[0:1, NE:NE + 1], min_val=NE, max_val=MAX_BLOCKS)
                dve.wait_ge(m.hidT_h, total + 1)
                hidT()
                dve.wait_ge(m.down, total + 1)
                dve.wait_ge(m.y_out, total * 16 + 16)
                output()
                dve.wait_ge(x_back, 16 * NT * (l + 1))

            def combine(m, i):
                for n, w in enumerate((w_lo, w_hi)):
                    buf = 2 * (i % 2) + n
                    dve.wait_ge(m.got[buf], m.got_base + 16 * (i // 2 + 1))
                    op = V.scalar_tensor_tensor(xr[:, i, :], got[buf], w[:, i:i + 1], xr[:, i, :], ALU.mult, ALU.add)
                    if n:
                        op.then_inc(m.x, 1)
                    else:
                        ch(op)

            moe(layers[0])
            gate_rows(1, range(2))

            def norm_tile(i):
                if i >= 2:
                    dve.wait_ge(a_T1, i - 1)
                dve.wait_ge(rstd_ok, 1 + NT + i + 1)
                normalise(xn_t[i % 2][:], i).then_inc(a_xn, 1)

            def rotate(dst1, dst2, x1, x2, cs, sn, t):
                ch(V.tensor_tensor(t[0], x1, cs, ALU.mult))
                ch(V.tensor_tensor(t[1], x2, sn, ALU.mult))
                ch(V.tensor_tensor(dst1, t[0], t[1], ALU.subtract))
                ch(V.tensor_tensor(t[0], x1, sn, ALU.mult))
                ch(V.tensor_tensor(t[1], x2, cs, ALU.mult))
                ch(V.tensor_tensor(dst2, t[0], t[1], ALU.add))

            def latents(i):
                u = i % 2
                if i >= 2:
                    dve.wait_ge(a_T2, i - 1)
                dve.wait_ge(a_r, i + 1)
                ch(V.tensor_scalar(lat[u][:, 0:2, :].rearrange("p a b -> p (a b)"), ps[:, 2, 0:KVR], sm[:, 18:19], None, ALU.mult))
                R2 = ROPE // 2
                twice = lat[u][:, 2, :].rearrange("p (c s n) -> p s c n", c=2, s=2)

                def both(v):
                    return v.unsqueeze(1).to_broadcast([P, 2, R2])

                t = [rope_t[:, n, 0:2, :] for n in range(2)]
                rotate(twice[:, 0], twice[:, 1], both(ps[:, 2, KVR:KVR + R2]), both(ps[:, 2, KVR + R2:KVR + ROPE]),
                       both(cosr[:, i, :]), both(sinr[:, i, :]), t)
                V.tensor_scalar(cqn[u][:].rearrange("p a b -> p (a b)"), ps[:, 3, 0:QR], sm[:, 19:20], None, ALU.mult).then_inc(a_nrm, 1)

            def rotate_q(i):
                u = i % 2
                R2 = ROPE // 2
                if i >= 2:
                    dve.wait_ge(a_T3, i - 1)
                dve.wait_ge(a_R, i + 1)
                x = ps[:, 6, :].rearrange("p (h n) -> p h n", n=ROPE)

                def heads(v):
                    return v.unsqueeze(1).to_broadcast([P, NH, R2])

                rotate(qro[u][:, :, 0:R2], qro[u][:, :, R2:], x[:, :, 0:R2], x[:, :, R2:], heads(cosr[:, i, :]), heads(sinr[:, i, :]),
                       [rope_t[:, 2 + n] for n in range(2)])
                V.memset(sm[:, 42:43], 0.0).then_inc(a_qr, 1)

            dve.wait_ge(trig_ok, 2)
            combine(layers[0], 0)
            combine(layers[0], 1)
            norm_tile(0)
            combine(layers[0], 2)
            norm_tile(1)
            for i in range(NT + 1):
                if i + 3 < NT:
                    combine(layers[0], i + 3)
                if i + 2 < NT:
                    norm_tile(i + 2)
                if i < NT:
                    latents(i)
                if i >= 1:
                    rotate_q(i - 1)
            for n in range(2 * NT):
                i, half = divmod(n, 2)
                dve.wait_ge(v_ps, n + 1)
                V.tensor_copy(v_all[:, i, 4 * half:4 * half + 4, :].rearrange("p h n -> p (h n)"), ps[:, 2 + n % 2, :]).then_inc(v_ev, 1)

            def maxima(u):
                i, h = UNITS[u]
                n = (i + 1) * P
                s = banks(2 * (u % 2))
                dve.wait_ge(s_ok, u + 1)
                ch(V.tensor_tensor(s[:, i * P:n], s[:, i * P:n], causal[:], ALU.add))
                ch(V.tensor_reduce(sm[:, 12 + u % 2:13 + u % 2], s[:, 0:n], AX_X, ALU.max))
                V.tensor_scalar(sm[:, 4 + u % 4:5 + u % 4], sm[:, 12 + u % 2:13 + u % 2], -ATTN_SCALE, None, ALU.mult).then_inc(nb_ok, 1)

            def outputs(u):
                i, h = UNITS[u]
                dve.wait_ge(p_ok, u + 1)
                ch(V.reciprocal(sm[:, 20 + u % 2:21 + u % 2], sm[:, 8 + u % 4:9 + u % 4]))
                dve.wait_ge(o_ps, u + 1)
                V.tensor_scalar(scratch[:, h * P:(h + 1) * P], ps[:, 6 + u % 2, 0:P], sm[:, 20 + u % 2:21 + u % 2], None, ALU.mult).then_inc(o_ok, 1)

            def out_T(i):
                dve.wait_ge(o_T, i + 1)
                V.tensor_copy(qT[:, 4:8, i * P:(i + 1) * P], ps[:, 7, :].rearrange("p (k n) -> p k n", n=P)).then_inc(oT_v, 1)

            for u in range(len(UNITS) + 2):
                if u < len(UNITS):
                    maxima(u)
                if 1 <= u <= len(UNITS):
                    i, h = UNITS[u - 1]
                    dve.wait_ge(pT_ps, u)
                    if i >= 4:
                        V.tensor_copy(probsT[(u - 1) % 2][:, 4:i + 1, :].rearrange("p a b -> p (a b)"),
                                      ps[:, 5, 0:(i - 3) * P]).then_inc(pT_v, 1)
                if u >= 2:
                    i, h = UNITS[u - 2]
                    if h == 0 and i:
                        out_T(i - 1)
                    outputs(u - 2)
            out_T(NT - 1)
            gate_rows(1, range(2, 4))
            dve.wait_ge(row_ok, 8)
            for n in range(NT + 1):
                if n:
                    modulated(layers[1], n - 1)
                if n < NT:
                    dve.wait_ge(mid_in[n // 4], 64)
                    for half in range(2):
                        add_mixed(WO_ORDER[n], half, mix_t2, m_ps, 2 * n + half + 1, m_ev)
            moe(layers[1])
            dve.wait_ge(misc_in, 64)
            for i in range(NT):
                if i == 0:
                    combine(layers[1], 0)
                if i + 1 < NT:
                    combine(layers[1], i + 1)
                dve.wait_ge(rstd_ok, 3 * NT + 1 + i + 1)
                if i >= 2:
                    dve.wait_ge(out_done[i % 2], 16 * (i // 2))
                V.scalar_tensor_tensor(fin[i % 2][:], xr[:, i, :], rstd[:, i:i + 1], final_row[:], ALU.mult, ALU.mult).then_inc(f_ok, 1)

        @block.tensor
        def _(pe):
            def T(dst, src, n=P):
                return nc.tensor.transpose(dst, src, ident[0:n, 0:n])

            def mm(dst, w, x, first, last):
                return nc.tensor.matmul(dst, w, x, start=first, stop=last)

            pe.wait_ge(consts_ok, 3)
            pe.wait_ge(vec_in, 16 * (len(VEC_ROWS) + 4))
            T(ps[:, 7, 0:NVEC], vec_rows[0:NVEC, 0, :], NVEC)
            T(ps[:, 7, COL_ADA_B:COL_ADA_B + 96], vec_rows[0:96, 1, :], 96)
            for u in range(2):
                T(ps[:, 7, COL_DW + u * DW_ROWS:COL_DW + (u + 1) * DW_ROWS], vec_rows[0:DW_ROWS, 2 + u, :], DW_ROWS)
            pe.wait_ge(dve_own, 1)
            T(ps[:, 7, COL_POS:COL_POS + NT], pos_rows_f[0:NT, :], NT).then_inc(vec_T, 1)

            def ada(slot, n_in, dst):
                pe.wait_ge(ada_in[slot], n_in)
                for t in range(2):
                    for k in range(KD):
                        last = mm(dst(t), ada_w[slot][:, k, t, :], c_col[:, k:k + 1], k == 0, k == KD - 1)
                last.then_inc(ada_used, 1)

            pe.wait_ge(c_ok, 1)
            for g in range(ADA_FIRST):
                ada(g % ADA_SLOTS, 16 * (g // ADA_SLOTS + 1), lambda t: ps[:, 6, 2 * g + t:2 * g + t + 1])
            for n in range(2 * KD):
                g, k = divmod(n, KD)
                pe.wait_ge(xn_ok, 4 * (g + 1))
                if n >= 4:
                    pe.wait_ge(hT_ok, n - 3)
                for t in range(4):
                    last = T(ps[:, n % 4, t * P:(t + 1) * P], v_tok[:, 4 * g + t, k * P:(k + 1) * P])
                last.then_inc(in_T, 1)
            pe.wait_ge(hT_ok, 2 * KD)

            def conv_in(c, u):
                pe.wait_ge(win_in[u], (c - u) * 16 + 32)
                for half in range(2):
                    pe.wait_ge(uv_free, 2 * c + half + 1)
                    for g in range(2):
                        for k in range(KD):
                            last = mm(ps[:, 2 * half + g, :], w_in[u][:, k, g, :], hT[:, k, half * HALF:(half + 1) * HALF],
                                      k == 0, k == KD - 1)
                    last.then_inc(uv_ready, 1)
                for n in range(ADA_PER_C):
                    g = ADA_FIRST + n
                    ada(g % ADA_SLOTS, c * 16 + 16 * (g // ADA_SLOTS + 1),
                        lambda t: ps[:, 7, bass.ds(c * (2 * ADA_PER_C) + (2 * n + t), 1)])

            def conv_T_tile(c, u):
                pe.wait_ge(tap_done, 2 * TAPS * c + 2 * TAPS)
                pe.wait_ge(conv_ev, 2 * c + 2)
                for half in range(2):
                    for t in range(4):
                        last = T(ps[:, 4 + half, t * P:(t + 1) * P], acc[u][:, (4 * half + t) * P:(4 * half + t + 1) * P])
                    last.then_inc(conv_T, 1)

            conv_in(0, 0)
            with pe.Fori(0, KD // 2 - 1) as j:
                for u in range(2):
                    conv_in(2 * j + (u + 1), 1 - u)
                    conv_T_tile(2 * j + u, u)
            conv_in(KD - 1, 1)
            conv_T_tile(KD - 2, 0)
            conv_T_tile(KD - 1, 1)

            def gate_rows(l, rs):
                for r in rs:
                    if r >= 2:
                        pe.wait_ge(row_ok, 4 * l + r - 1)
                    for k in range(KD):
                        pe.wait_ge(diag_ok, KD * (4 * l + r) + k + 1)
                        last = mm(ps[:, 4 + 2 * (r % 2) + k // 4, (k % 4) * P:(k % 4 + 1) * P], ones[:], scratch[:, k * P:(k + 1) * P], True, True)
                    last.then_inc(row_ps, 1)

            pe.wait_ge(mod_ok, 1)
            pe.wait_ge(conv_ev, 2 * KD + 2)
            gate_rows(0, range(4))
            pe.wait_ge(row_ok, 4)
            pe.wait_ge(wout_in, 16)

            def vn_tile(i):
                pe.wait_ge(vn_ok, i + 1)
                if i:
                    pe.wait_ge(vT_ok, KD * i)
                for k in range(KD):
                    last = T(banks(0)[:, k * P:(k + 1) * P], v_tok[:, i, k * P:(k + 1) * P])
                last.then_inc(vn_T, 1)

            def route(m, n):
                if 1 <= n <= NT:
                    i = TILE_ORDER[m.l][n - 1]
                    pe.wait_ge(m.xn, n)
                    if n >= 2:
                        pe.wait_ge(m.h2T, n - 1)
                    for k in range(KD):
                        last = T(banks(2)[:, k * P:(k + 1) * P], h_rows[:, i, k * P:(k + 1) * P])
                    last.then_inc(m.T, 1)
                if 2 <= n <= NT + 1:
                    i = TILE_ORDER[m.l][n - 2]
                    pe.wait_ge(m.h2T, n - 1)
                    for k in range(KD):
                        last = mm(ps[:, 6, i * NE:(i + 1) * NE], h2T[n % 2][:, k, :], router[:, k, :], k == 0, k == KD - 1)
                    last.then_inc(m.logit, 1)

            vn_tile(0)
            for n in range(NT + 2):
                if n + 1 < NT:
                    vn_tile(n + 1)
                if n < NT:
                    pe.wait_ge(vT_ok, KD * (n + 1))
                    for half in range(2):
                        if n:
                            pe.wait_ge(mixed, 2 * (n - 1) + half + 1)
                        for k in range(KD):
                            last = mm(ps[:, 4 + half, :], vT[n % 2][:, k, :], w_out[:, k, half * HALF:(half + 1) * HALF],
                                      k == 0, k == KD - 1)
                        last.then_inc(mix_ok, 1)
                route(layers[0], n)

            def moe(m):
                pe.wait_ge(m.mask, 1)
                mm(ps[:, 7, 0:P], before[:], rt[:, 4, :], True, True)
                mm(ps[:, 7, P:2 * P], ones[:], rt[:, 4, :], True, True).then_inc(m.rank, 1)

                def rows_T(b):
                    pe.wait_ge(m.rows_in, b * 16 + 16)
                    for k in range(KD):
                        last = T(banks(2)[:, k * P:(k + 1) * P], rows[:, k * P:(k + 1) * P])
                    last.then_inc(m.rows_T, 1)

                pe.wait_ge(m.plan, 1)
                rows_T(0)

                def three(dst, xh, xl, wh, wl, k, nk):
                    mm(dst, xh, wh, k == 0, False)
                    mm(dst, xh, wl, False, False)
                    return mm(dst, xl, wh, False, k == nk - 1)

                def wide(n, bank):
                    wh, wl = (v[n][:].rearrange("p c (k n) -> p (c k) n", n=DE) for v in (part_h, part_l))
                    for k in range(KD):
                        last = three(ps[:, bank, :], rowsT_h[:, k, :], rowsT_l[:, k, :], wh[:, k, :], wl[:, k, :], k, KD)
                    return last

                def hid_T():
                    for k in range(DE // P):
                        last = T(ps[:, 4, k * P:(k + 1) * P], hid[:, k * P:(k + 1) * P])
                    last.then_inc(m.hid_T, 1)

                def down():
                    for half in range(2):
                        sl = slice(half * HALF, (half + 1) * HALF)
                        for k in range(DE // P):
                            last = three(ps[:, 5 + half, :], hidT_h[:, k, :], hidT_l[:, k, :], part_h[2][:, k, sl], part_l[2][:, k, sl],
                                         k, DE // P)
                    last.then_inc(m.down, 1)

                with pe.Fori(0, NE) as e:
                    first = pe.value_load(starts[0:1, bass.ds(e, 1)], min_val=0, max_val=MAX_BLOCKS)
                    end = pe.value_load(starts[0:1, bass.ds(e + 1, 1)], min_val=1, max_val=MAX_BLOCKS)
                    with pe.Fori(first, end) as b:
                        pe.wait_ge(m.lo[0], e * PIECES + (m.n_split + PIECES))
                        pe.wait_ge(m.rowsT_l, b + 1)
                        wide(0, 0).then_inc(m.gate, 1)
                        pe.wait_ge(m.hid, b + 1)
                        hid_T()
                        pe.wait_ge(m.lo[1], e * PIECES + (m.n_split + PIECES))
                        wide(1, 1).then_inc(m.up, 1)
                        rows_T(b + 1)
                        pe.wait_ge(m.hidT_l, b + 1)
                        pe.wait_ge(m.lo[2], e * PIECES + (m.n_down + PIECES))
                        pe.wait_ge(m.y, b + 1)
                        down()
                total = pe.value_load(starts[0:1, NE:NE + 1], min_val=NE, max_val=MAX_BLOCKS)
                pe.wait_ge(m.hid, total + 1)
                hid_T()
                pe.wait_ge(m.hidT_l, total + 1)
                pe.wait_ge(m.y, total + 1)
                down()

            moe(layers[0])
            gate_rows(1, range(2))
            pe.wait_ge(row_ok, 6)

            def T1(i):
                pe.wait_ge(a_xn, i + 1)
                if i:
                    pe.wait_ge(a_xnT, i)
                for k in range(KD):
                    last = T(banks(0)[:, k * P:(k + 1) * P], xn_t[i % 2][:, k * P:(k + 1) * P])
                last.then_inc(a_T1, 1)

            def M(i):
                pe.wait_ge(a_xnT, i + 1)
                if i:
                    pe.wait_ge(a_nrm, i)
                for k in range(KD):
                    mm(ps[:, 2, 0:KVR + ROPE], xnT[i % 2][:, k, :], w_dkv[:, k, :], k == 0, k == KD - 1)
                for k in range(KD):
                    last = mm(ps[:, 3, 0:QR], qinT[i % 2][:, k, :], w_dq[:, k, :], k == 0, k == KD - 1)
                last.then_inc(a_M, 1)

            def T2(i):
                pe.wait_ge(a_nrm, i + 1)
                for k in range(3):
                    T(ps[:, 4, k * P:(k + 1) * P], lat[i % 2][:, k, :])
                for k in range(3):
                    last = T(ps[:, 5, k * P:(k + 1) * P], cqn[i % 2][:, k, :])
                last.then_inc(a_T2, 1)

            def rope_q(i):
                pe.wait_ge(a_ev2, 3 * (i + 1))
                if i:
                    pe.wait_ge(a_qr, i)
                for k in range(QR // P):
                    last = mm(ps[:, 6, :], cqT[:, k, i * P:(i + 1) * P], w_uqr[:, k].rearrange("p h n -> p (h n)"), k == 0, k == QR // P - 1)
                last.then_inc(a_R, 1)

            def T3(i):
                pe.wait_ge(a_qr, i + 1)
                if i:
                    pe.wait_ge(a_ev3, i)
                x = qro[i % 2][:].rearrange("p h n -> p (h n)")
                for k in range(NH // 2):
                    last = T(ps[:, 7, k * P:(k + 1) * P], x[:, k * P:(k + 1) * P])
                last.then_inc(a_T3, 1)

            T1(0)
            pe.wait_ge(folded, KD)
            pe.wait_ge(aw_in[1], 16)
            for i in range(NT + 2):
                if i + 1 < NT:
                    T1(i + 1)
                if i < NT:
                    M(i)
                if 1 <= i <= NT:
                    T2(i - 1)
                    if i == 1:
                        pe.wait_ge(folded, KD + QR // P)
                    rope_q(i - 1)
                if i >= 2:
                    T3(i - 2)
            pe.wait_ge(a_ev3, NT)
            pe.wait_ge(folded, KD + QR // P + KVR // P)
            for n in range(2 * NH):
                h, half = divmod(n, 2)
                if n >= 2:
                    pe.wait_ge(k_ev, n - 1)
                for k in range(KVR // P):
                    last = mm(ps[:, n % 2, :], w_ukv[:, k, h, 0, :], latT[:, k, half * HALF:(half + 1) * HALF], k == 0, k == KVR // P - 1)
                last.then_inc(k_ps, 1)
            for n in range(2 * NT):
                i, half = divmod(n, 2)
                if n >= 2:
                    pe.wait_ge(v_ev, n - 1)
                for k in range(KVR // P):
                    last = mm(ps[:, 2 + n % 2, :], latT[:, k, i * P:(i + 1) * P], w_ukv[:, k, 4 * half:4 * half + 4, 1, :], k == 0, k == KVR // P - 1)
                last.then_inc(v_ps, 1)
            pe.wait_ge(folded, KD + 2 * (QR // P) + KVR // P)
            for n in range(2 * NH):
                h, half = divmod(n, 2)
                if n >= 2:
                    pe.wait_ge(q_ev, n - 1)
                for k in range(QR // P):
                    last = mm(ps[:, 4 + n % 2, :], w_uqn[:, k, h, :], cqT[:, k, half * HALF:(half + 1) * HALF], k == 0, k == QR // P - 1)
                last.then_inc(q_ps, 1)
            pe.wait_ge(k_ev, 2 * NH)
            pe.wait_ge(v_ev, 2 * NT)
            pe.wait_ge(q_ev, 2 * NH)

            def scores(u):
                i, h = UNITS[u]
                n = (i + 1) * P
                if u >= 2:
                    pe.wait_ge(p_ok, u - 1)
                half_p = slice(ROPE * (h % 2), ROPE * (h % 2) + ROPE)
                tok = slice(i * P, (i + 1) * P)
                for c in range(0, n, HALF):
                    w = min(HALF, n - c)
                    dst = ps[:, 2 * (u % 2) + c // HALF, 0:w]
                    mm(dst, qT[:, h, tok], kT[:, h, c:c + w], True, False)
                    last = mm(dst, qrT[half_p, h // 2, tok], krT[half_p, c:c + w], False, True)
                last.then_inc(s_ok, 1)

            def probs_T(u):
                i, h = UNITS[u]
                pe.wait_ge(p_ok, u + 1)
                if u:
                    pe.wait_ge(pT_a, u)
                    if UNITS[u - 1][0] >= 4:
                        pe.wait_ge(pT_v, u - 4 * NH)
                for j in range(i + 1):
                    last = T(ps[:, 4 + j // 4, (j % 4) * P:(j % 4 + 1) * P], probs[u % 2][:, j * P:(j + 1) * P])
                last.then_inc(pT_ps, 1)

            def out_T(i):
                pe.wait_ge(o_ok, NH * (i + 1))
                for k in range(NH):
                    last = T(ps[:, 6 + k // 4, (k % 4) * P:(k % 4 + 1) * P], scratch[:, k * P:(k + 1) * P])
                last.then_inc(o_T, 1)

            def output(u):
                i, h = UNITS[u]
                pe.wait_ge(pT_a, u + 1)
                if i >= 4:
                    pe.wait_ge(pT_v, u - 4 * NH + 1)
                if u >= 2:
                    pe.wait_ge(o_ok, u - 1)
                if h < 2 and i:
                    pe.wait_ge(oT_a, i)
                    pe.wait_ge(oT_v, i)
                for j in range(i + 1):
                    last = mm(ps[:, 6 + u % 2, 0:P], probsT[u % 2][:, j, :], v_all[:, j, h, :], j == 0, j == i)
                last.then_inc(o_ps, 1)

            scores(0)
            for u in range(len(UNITS) + 1):
                if u + 1 < len(UNITS):
                    scores(u + 1)
                if u < len(UNITS):
                    probs_T(u)
                if u:
                    i, h = UNITS[u - 1]
                    if h == 0 and i:
                        out_T(i - 1)
                    output(u - 1)
            out_T(NT - 1)
            pe.wait_ge(oT_a, NT)
            pe.wait_ge(oT_v, NT)
            pe.wait_ge(aw_in[5], 16)
            gate_rows(1, range(2, 4))
            pe.wait_ge(row_ok, 8)
            for n in range(NT + 2):
                if n < NT:
                    i = WO_ORDER[n]
                    for half in range(2):
                        if n:
                            pe.wait_ge(m_ev, 2 * (n - 1) + half + 1)
                        for h in range(NH):
                            last = mm(ps[:, 4 + half, :], qT[:, h, i * P:(i + 1) * P], w_o[:, h, half * HALF:(half + 1) * HALF],
                                      h == 0, h == NH - 1)
                        last.then_inc(m_ps, 1)
                route(layers[1], n)
            moe(layers[1])


class Count:

    def __init__(self, engine, own):
        self.engine, self.own, self.n = engine, own, 0

    def chain(self, instruction):
        self.n += 1
        instruction.then_inc(self.own, 1)
        self.engine.wait_ge(self.own, self.n)


INPUTS = ["x", "c", "positions", "ada_w", "ada_b", "norm1_g", "norm2_g", "conv_w_in", "conv_b_in", "conv_w_dw", "conv_b_dw",
          "conv_ln_g", "conv_ln_b", "conv_w_out", "kv_in_g", "w_dkv", "kv_norm_g", "w_ukv", "w_dq", "q_norm_g", "w_uq", "w_o",
          "router_w", "router_b", "exp_w_gate", "exp_w_up", "exp_w_down", "final_g"]


def kernel(**inputs):
    import concourse.bacc as bacc
    from concourse.bass_utils import run_bass_kernel_spmd

    nc = bacc.Bacc("TRN2", target_bir_lowering=False, num_devices=1)
    arrays = {f"in_{n}": np.ascontiguousarray(inputs[n]) for n in INPUTS}
    arrays["in_inv_freq"] = (np.float32(10000.0) ** (-np.arange(0, ROPE, 2, dtype=np.float32) / np.float32(ROPE))).astype(np.float32)
    aps = {n[3:]: nc.dram_tensor(n, v.shape, mybir.dt.from_np(v.dtype), kind="ExternalInput").ap() for n, v in arrays.items()}
    out = nc.dram_tensor("out", (1, S, D), F32, kind="ExternalOutput").ap()
    build_trunk(nc, aps, out)
    r = run_bass_kernel_spmd(nc, [arrays], core_ids=[0])
    return r.results[0]["out"]
```

```python
from contextlib import ExitStack

import concourse.bass as bass
import numpy as np
from concourse import mybir

F32 = mybir.dt.float32
F32R = mybir.dt.float32r
I32 = mybir.dt.int32
ALU = mybir.AluOpType
ACT = mybir.ActivationFunctionType
AX_X = mybir.AxisListType.X

P = 128
D = 1024
S = 1024
KD = D // P
NT = S // P
HALF = 512
TAPS = 31
PAD = TAPS - 1
SIDE_TAPS = 9
NH = 8
NOPE = 128
ROPE = 64
QR = 384
KVR = 256
NE = 16
NG = 4
EPG = NE // NG
DE = 512
EPS = 1e-6
NEG = -1e30
ATTN_SCALE = 1.0 / float(np.sqrt(NOPE + ROPE))
MAX_BLOCKS = 2 * S // P + NE
ROW_BLOCKS = MAX_BLOCKS + 3

VEC_ROWS = [("c", 8), ("norm1_g", 16), ("norm2_g", 16), ("kv_in_g", 8), ("conv_b_in", 16), ("conv_b_dw", 8),
            ("conv_ln_g", 8), ("conv_ln_b", 8), ("kv_norm_g", 2), ("q_norm_g", 3)]
COL = {}
_at = 0
for _name, _n in VEC_ROWS:
    COL[_name] = _at
    _at += _n
NVEC = _at
COL_ADA_B = 96
COL_DW = 192
DW_ROWS = TAPS * KD // 2
COL_POS = COL_DW + 2 * DW_ROWS
NCOL = COL_POS + NT
ADA_Q = 4
ADA_CHUNKS = 6 * ADA_Q
ADA_EARLY = 8
ADA_FIRST = 2 * ADA_Q
ADA_PER_C = (ADA_CHUNKS - ADA_FIRST) // KD
ADA_SLOTS = 3
ADA_N = 256


def ada_slot(g):
    if g < ADA_FIRST:
        return g % ADA_SLOTS, g // ADA_SLOTS + 1
    c, n = divmod(g - ADA_FIRST, ADA_PER_C)
    slot = n % ADA_SLOTS
    return slot, sum(ada_slot(h)[0] == slot for h in range(ADA_FIRST)) + c * ada_per_c(slot) + n // ADA_SLOTS + 1


def ada_per_c(slot):
    return len(range(slot, ADA_PER_C, ADA_SLOTS))


TWO_PI = 2 * np.pi
C1 = 6.28125
C2 = float(np.float32(np.float16(TWO_PI - C1)))
C3 = float(TWO_PI - C1 - C2)
ROUND = 1.5 * 2.0 ** 23


def build_trunk(nc, a, out):
    sorted_rows = nc.dram_tensor("sorted_rows", (ROW_BLOCKS * P, D), F32, kind="Internal").ap()
    x_res = [nc.dram_tensor(f"x_res{l}", (S, D), F32, kind="Internal").ap() for l in range(2)]
    x_mid = nc.dram_tensor("x_mid", (S, D), F32, kind="Internal").ap()

    ada_out = nc.dram_tensor("ada_out", (1, ADA_CHUNKS * ADA_N), F32, kind="Internal").ap()

    ada_parts = nc.dram_tensor("ada_parts", (P, ADA_CHUNKS * ADA_N), F32, kind="Internal").ap()

    with ExitStack() as ctx:
        def sb(name, *shape, dt=F32):
            return ctx.enter_context(nc.sbuf_tensor(name, [P, *shape], dt))

        def sem(name):
            return ctx.enter_context(nc.semaphore(name))

        def sems(name, n):
            return [sem(f"{name}{i}") for i in range(n)]

        ident = sb("ident", P)
        before = sb("before", P)
        ones = sb("ones", P)
        causal = sb("causal", P)
        cols = sb("cols", NCOL)
        modc = sb("modc", 96)
        gainc = sb("gainc", 4, KD)
        gate_row = sb("gate_row", 2, D)
        scratch = sb("scratch", D)
        cosr = sb("cosr", NT, ROPE // 2)
        sinr = sb("sinr", NT, ROPE // 2)
        invf = sb("invf", ROPE // 2)
        c_col = sb("c_col", KD)
        ssq = sb("ssq", NT)
        rstd = sb("rstd", NT)
        mv = sb("mv", NT, 2)
        bst = sb("bst", 2 * NT, 6)
        neghalf = sb("neghalf", NT)
        router = sb("router", KD, NE)
        router_bias = sb("router_bias", NE)
        rt = sb("rt", 12, P)
        rcol = sb("rcol", 8, NT)
        w_lo = sb("w_lo", NT)
        w_hi = sb("w_hi", NT)
        d_lo = sb("d_lo", NT, dt=I32)
        d_hi = sb("d_hi", NT, dt=I32)
        starts = sb("starts", NE + 1, dt=I32)
        sm = sb("sm", 48)
        g_lo = sb("g_lo", NT, dt=I32)
        g_hi = sb("g_hi", NT, dt=I32)
        ps = ctx.enter_context(nc.psum_tensor("ps", [P, 8, HALF], F32))

        base = -(-nc.sbuf_base // 64) * 64
        X_SIZE = NT * D
        room = (nc.sbuf_usable_end - base) // 4 - X_SIZE

        def at(name, offset, *shape, dt=F32):
            assert offset + int(np.prod(shape)) <= room, (name, offset, shape, room)
            return nc.alloc_sbuf_tensor_at(name, [P, *shape], dt, offset=base + 4 * (offset + X_SIZE))

        xr = at("xr", -X_SIZE, NT, D)
        vec_rows = at("vec_rows", 0, 4, P)
        pos_rows = at("pos_rows", 4 * P, P, dt=I32)
        pos_rows_f = at("pos_rows_f", 5 * P, P)
        hT_h = at("hT_h", 0, KD, S, dt=F32R)
        hT_l = at("hT_l", -X_SIZE, KD, S, dt=F32R)
        w_in = [at(f"w_in{u}", 8192 + 2048 * u, KD, 2, P) for u in range(2)]
        ada_w = [at(f"ada_w{s}", 12288 + 2048 * s, KD, ADA_N) for s in range(ADA_SLOTS)]
        w_in_h = at("w_in_h", 18432, KD, 2, P, dt=F32R)
        w_in_l = at("w_in_l", 20480, KD, 2, P, dt=F32R)
        w_out = at("w_out", 4096, KD, D)
        glu = at("glu", 22528, PAD + S)
        sig = at("sig", 23584, 2, HALF)
        acc = [at(f"acc{u}", 24640 + S * u, S) for u in range(2)]
        vT = [at(f"vT{u}", 26688 + D * u, KD, P) for u in range(2)]
        v_tok = at("v_tok", 28800, NT, D)
        ada_row = at("ada_row", 26688, ADA_FIRST * ADA_N)
        mod_rows = at("mod_rows", 37568, P)
        mix_t = at("mix_t", 24640, D)
        ZERO_N = ROW_BLOCKS * D // KD // 8
        zero = at("zero", 36992, ZERO_N)
        angle = [at(f"angle{n}", 24640 + 256 * n, NT, ROPE // 2) for n in range(4)]
        raw = [at(f"raw_{n}", 4096 * n - X_SIZE, 4, 1024) for n in range(3)]
        part_h = [at(f"w{n}_h", 4096 + 8192 * n, 4, 1024, dt=F32R) for n in range(3)]
        part_l = [at(f"w{n}_l", 8192 + 8192 * n, 4, 1024, dt=F32R) for n in range(3)]
        h_rows = at("h_rows", 12288, NT, D)
        mod_row = at("mod_row", 22528, 2, D)
        h2T = [at(f"h2T{u}", 20480 + D * u, KD, P) for u in range(2)]
        rows = at("rows", 28672, D)
        rowsT_h = at("rowsT_h", 29696, KD, P, dt=F32R)
        rowsT_l = at("rowsT_l", 30720, KD, P, dt=F32R)
        act = at("act", 31744, DE)
        hid = at("hid", 32256, DE)
        hidT_h = at("hidT_h", 32768, DE // P, P, dt=F32R)
        hidT_l = at("hidT_l", 33280, DE // P, P, dt=F32R)
        y_sb = at("y_sb", 33792, D)
        got = [at(f"got{n}", 21504 + D * n, D)[:] for n in range(3)] + [rt[:, 0:8, :].rearrange("p a b -> p (a b)")]
        ada_x = at("ada_x", 34816, KD, ADA_N)
        ada_x0 = [at(f"ada_x0{u}", KD * ADA_N * u, KD, ADA_N) for u in range(2)]
        pool_mark = at("pool_mark", 37568, 1)
        ada_p = at("ada_p", 24576, 5 * D)
        ada_p5 = at("ada_p5", 32768, D)
        fin = [at(f"fin{n}", 8192 + D * n, D) for n in range(2)]
        got_last = [at(f"got_last{n}", 11264 + D * n, D)[:] for n in range(8)]
        final_row = at("final_row", 10240, D)
        xn_t = [at(f"xn_t{u}", 8192 + D * u, D) for u in range(2)]
        xnT = [at(f"xnT{u}", 10240 + D * u, KD, P) for u in range(2)]
        qinT = [at(f"qinT{u}", 12288 + D * u, KD, P) for u in range(2)]
        lat = [at(f"lat{u}", 14336 + 384 * u, 3, P) for u in range(2)]
        cqn = [at(f"cqn{u}", 15104 + 384 * u, 3, P) for u in range(2)]
        qro = [at(f"qro{u}", 15872 + 512 * u, NH, ROPE) for u in range(2)]
        rope_t = at("rope_t", 16896, 4, NH, ROPE // 2)
        w_dq = at("w_dq", 18432, KD, QR)
        w_ukv = at("w_ukv", 0, KVR // P, NH, 2, P)
        w_dkv = at("w_dkv", 4096, KD, KVR + ROPE)
        w_uqr = at("w_uqr", 6656, QR // P, NH, ROPE)
        latT = at("latT", 24576, KVR // P, S)
        cqT = at("cqT", 26624, QR // P, S)
        w_uqn = at("w_uqn", 29696, QR // P, NH, P)
        kT = at("kT", 16384, NH, S)
        v_all = at("v_all", 8192, NT, NH, P)
        qT = at("qT", 0, NH, S)
        w_o = at("w_o", 24576, NH, D)
        krT = at("krT", 32768, S)
        qrT = at("qrT", 33792, NH // 2, S)
        mix_t2 = at("mix_t2", 33792, D)
        xflat = xr[:].rearrange("p a b -> p (a b)")
        probs = [xflat[:, S * u:S * (u + 1)] for u in range(2)]
        probsT = [xflat[:, 2048 + S * u:2048 + S * (u + 1)].rearrange("p (a b) -> p a b", b=P) for u in range(2)]

        consts_ok, vec_in, vec_T, vec_ok, c_ok = sem("consts_ok"), sem("vec_in"), sem("vec_T"), sem("vec_ok"), sem("c_ok")
        x_in = sems("x_in", 2)
        misc_in, zeroed = sem("misc_in"), sem("zeroed")
        ada_in, ada_used = sems("ada_in", ADA_SLOTS), sem("ada_used")
        ada_ev, ada_saved, ada_back, mod_T = sem("ada_ev"), sem("ada_saved"), sem("ada_back"), sem("mod_T")
        mod_first, mod_ok = sem("mod_first"), sem("mod_ok")
        win_hi, win_lo, hT_lo = sem("win_hi"), sem("win_lo"), sem("hT_lo")
        win_in, wout_in = sems("win_in", 2), sem("wout_in")
        pool_own, dve_own = sem("pool_own"), sem("dve_own")
        ssq_ok, rstd_ok, xn_ok = sem("ssq_ok"), sem("rstd_ok"), sem("xn_ok")
        in_T, hT_ok = sem("in_T"), sem("hT_ok")
        uv_ready, sig_ok, uv_free, tap_done = sem("uv_ready"), sem("sig_ok"), sem("uv_free"), sem("tap_done")
        conv_T, conv_ev = sem("conv_T"), sem("conv_ev")
        side_ok, side_used, conv_sum = sem("side_ok"), sem("side_used"), sem("conv_sum")
        ln_ok, ln_rstd, vn_ok, vn_T, vT_ok, mix_ok, mixed = (sem("ln_ok"), sem("ln_rstd"), sem("vn_ok"), sem("vn_T"), sem("vT_ok"),
                                                             sem("mix_ok"), sem("mixed"))
        diag_ok, row_ps, row_ok = sem("diag_ok"), sem("row_ps"), sem("row_ok")
        ang_ok, trig_ok = sem("ang_ok"), sem("trig_ok")

        PIECES = 4
        weights_in, weights_hi, weights_lo = sems("w_in_", 3), sems("w_hi_", 3), sems("w_lo_", 3)
        x_back = sem("x_back")
        part_w, part_step, part_out, part_in = sem("part_w"), sem("part_step"), sem("part_out"), sems("part_in", 2)
        rows_got = sems("rows_got", 4)
        once = [sem(n) for n in ("m_score", "m_mask", "m_rank", "m_plan", "m_all_out", "m_saved", "m_scattered", "m_x", "m_h", "m_T", "m_h2T", "m_logit")]

        class Layer:

            def __init__(self, l):
                def s(n):
                    return sem(f"{n}_l{l}")
                self.l = l
                self.score, self.mask, self.rank, self.plan, self.all_out, self.saved, self.scattered, self.x, self.xn, self.T, self.h2T, self.logit = once
                self.turn = l + 1
                self.w_in, self.hi, self.lo = weights_in, weights_hi, weights_lo
                self.n_in, self.n_split = l * 16 * NE, l * PIECES * NE
                self.n_down = self.n_split + l * PIECES
                self.rows_in, self.rows_T, self.rowsT_h, self.rowsT_l = s("m_rows_in"), s("m_rows_T"), s("m_rowsT_h"), s("m_rowsT_l")
                self.gate, self.up, self.silu = s("m_gate"), s("m_up"), s("m_silu")
                self.hid, self.hid_T, self.hidT_h, self.hidT_l, self.down = s("m_hid"), s("m_hid_T"), s("m_hidT_h"), s("m_hidT_l"), s("m_down")
                self.y, self.y_out = s("m_y"), s("m_y_out")
                self.depth, self.bufs = (2, 4)[l], (got, got_last)[l]
                self.n_x = l * NT

        layers = [Layer(0), Layer(1)]
        mid_out, mid_in, out_done = sem("mid_out"), sems("mid_in", 2), sems("out_done", 2)
        aw_in = sems("aw_in", 6)
        folded = sem("folded")
        a_xn, a_T1, a_xnT, a_M, a_ss, a_r, a_nrm, a_T2, a_ev2, a_R, a_qr, a_T3, a_ev3 = (
            sem(f"a_{n}") for n in ("xn", "T1", "xnT", "M", "ss", "r", "nrm", "T2", "ev2", "R", "qr", "T3", "ev3"))
        k_ps, k_ev, v_ps, v_ev, q_ps, q_ev = (sem(n) for n in ("k_ps", "k_ev", "v_ps", "v_ev", "q_ps", "q_ev"))
        s_ok, nb_ok, p_ok, pT_ps, pT_a, pT_v, o_ps, o_ok, o_T, oT_a, oT_v, m_ps, m_ev = (
            sem(n) for n in ("s_ok", "nb_ok", "p_ok", "pT_ps", "pT_a", "pT_v", "o_ps", "o_ok", "o_T", "oT_a", "oT_v", "m_ps", "m_ev"))
        f_ok = sem("f_ok")

        UNITS = [(i, h) for i in range(NT) for h in range(NH)]
        WO_ORDER = [4, 5, 6, 7, 0, 1, 2, 3]
        TILE_ORDER = [list(range(NT)), WO_ORDER]

        def col(name, k, n=1):
            return cols[:, COL[name] + k:COL[name] + k + n]

        def mod(l, comp, k, n=1):
            at0 = l * 48 + comp * 8 + k
            return modc[:, at0:at0 + n]

        def banks(b):
            return ps[:, b:b + 2, :].rearrange("p b c -> p (b c)")

        def ada_src(g):
            return a["ada_w"][0].rearrange("(k p) n -> p k n", p=P)[:, :, g * ADA_N:(g + 1) * ADA_N]

        w_in_src = a["conv_w_in"][0].rearrange("(k p) (g c n) -> c p k g n", p=P, g=2, n=P)
        block = ctx.enter_context(nc.Block())

        @block.sync
        def _(sp):
            for name, n in VEC_ROWS:
                src = a[name]
                if len(src.shape) == 2:
                    src = src.rearrange("a b -> (a b)")
                sp.dma_start(vec_rows[COL[name]:COL[name] + n, 0, :], src.rearrange("(r n) -> r n", n=P)).then_inc(vec_in, 16)
            sp.dma_start(vec_rows[0:96, 1, :], a["ada_b"].rearrange("l (r n) -> (l r) n", n=P)).then_inc(vec_in, 16)
            dw = a["conv_w_dw"][0].rearrange("t (k n) -> (t k) n", n=P)
            for u in range(2):
                sp.dma_start(vec_rows[0:DW_ROWS, 2 + u, :], dw[u * DW_ROWS:(u + 1) * DW_ROWS, :]).then_inc(vec_in, 16)
            sp.dma_start(pos_rows[0:NT, :], a["positions"].rearrange("a (r n) -> (a r) n", n=P)).then_inc(vec_in, 16)
            xsrc = a["x"][0].rearrange("(t p) d -> t p d", p=P)
            for i in range(NT):
                sp.dma_start(xr[:, i, :], xsrc[i]).then_inc(x_in[i // 4], 16)

            def load_ada(g):
                slot = ada_slot(g)[0]
                before_g = [h for h in range(g) if ada_slot(h)[0] == slot]
                if before_g:
                    sp.wait_ge(ada_used, before_g[-1] + 1)
                sp.dma_start(ada_w[slot][:], ada_src(g)).then_inc(ada_in[slot], 16)

            sp.dma_start(invf[:], a["inv_freq"].partition_broadcast(P)).then_inc(misc_in, 16)
            sp.dma_start(router[:], a["router_w"].rearrange("(k p) e -> p k e", p=P)).then_inc(misc_in, 16)
            sp.dma_start(router_bias[:], a["router_b"].partition_broadcast(P)).then_inc(misc_in, 16)
            for g in range(ADA_FIRST):
                load_ada(g)

            def load_w_in(c):
                if c >= 2:
                    sp.wait_ge(win_lo, c - 1)
                for g in range(2):
                    sp.dma_start(w_in[c % 2][:, :, g, :], w_in_src[c][:, :, g, :]).then_inc(win_in[c % 2], 16)

            load_w_in(0)
            load_w_in(1)
            for c in range(KD):
                for g in range(ADA_FIRST + ADA_PER_C * c, ADA_FIRST + ADA_PER_C * (c + 1)):
                    load_ada(g)
                if c + 2 < KD:
                    load_w_in(c + 2)
            sp.wait_ge(uv_ready, 2 * KD)
            for i in range(NT):
                sp.dma_start(xr[:, i, :], xsrc[i]).then_inc(x_in[i // 4], 16)
            sp.dma_start(w_out[:], a["conv_w_out"][0].rearrange("(k p) d -> p k d", p=P)).then_inc(wout_in, 16)

            WEIGHTS = ("exp_w_gate", "exp_w_up", "exp_w_down")

            def load_matrix(m, n, e):
                nk = (KD, KD, DE // P)[n]
                src = a[WEIGHTS[n]][m.l].rearrange("e (k p) n -> p (e k) n", p=P)[:, bass.ds(e * nk, nk), :]
                dst = raw[n][:] if n == 2 else raw[n][:].rearrange("p c (k n) -> p (c k) n", n=DE)
                sp.dma_start(dst, src).then_inc(m.w_in[n], 16)

            def load_first(m):
                for n, i in enumerate(TILE_ORDER[m.l]):
                    sp.wait_ge((mixed, m_ev)[m.l], 2 * n + 2)
                    sp.dma_start(x_res[m.l][i * P:(i + 1) * P, :], xr[:, i, :]).then_inc(m.saved, 16)
                sp.wait_ge(m.saved, 16 * NT * m.turn)
                sp.wait_ge(m.xn, m.n_x + NT)
                sp.wait_ge(ssq_ok, (2 + 2 * m.l) * NT)
                for n in range(3):
                    if n == 2 and m.l:
                        sp.wait_ge(m_ps, 2 * NT)
                    elif n == 2:
                        sp.wait_ge(part_out, 16 * ADA_EARLY)
                    load_matrix(m, n, 0)

            def load_experts(m):
                def load(n, e):
                    before_n = m.n_down + PIECES if n == 2 else m.n_split
                    sp.wait_ge(m.lo[n], e * PIECES + before_n)
                    load_matrix(m, n, e)

                load(0, 1)
                load(1, 1)
                with sp.Fori(1, NE - 1) as e:
                    load(0, e + 1)
                    load(1, e + 1)
                    load(2, e)
                load(2, NE - 1)
                for n in range(3):
                    sp.wait_ge(m.lo[n], (m.n_down + PIECES if n == 2 else m.n_split) + PIECES * NE)
                for i in range(NT):
                    sp.dma_start(xr[:, i, :], x_res[m.l][i * P:(i + 1) * P, :]).then_inc(x_back, 16)

            m = layers[0]
            load_first(m)
            load_experts(m)
            sp.wait_ge(m.all_out, m.turn)
            sp.wait_ge(part_out, 16 * ADA_CHUNKS)
            sp.dma_start(ada_p[:, 0:2 * D], ada_parts[:, 0:2 * D]).then_inc(part_in[0], 16)
            sp.dma_start(w_dkv[:], a["w_dkv"].rearrange("(k p) n -> p k n", p=P)).then_inc(aw_in[0], 16)
            sp.dma_start(w_dq[:], a["w_dq"][0].rearrange("(k p) n -> p k n", p=P)).then_inc(aw_in[1], 16)
            sp.dma_start(ada_p[:, 2 * D:5 * D], ada_parts[:, 2 * D:5 * D]).then_inc(part_in[1], 16)
            sp.dma_start(ada_p5[:], ada_parts[:, 5 * D:6 * D]).then_inc(part_in[1], 16)
            uq = a["w_uq"][0].rearrange("(k p) (h n) -> p k h n", p=P, h=NH)
            for k in range(QR // P):
                sp.dma_start(w_uqr[:, k], uq[:, k, :, NOPE:]).then_inc(aw_in[2], 16)
                sp.dma_start(w_uqn[:, k], uq[:, k, :, 0:NOPE]).then_inc(aw_in[3], 16)
            sp.dma_start(w_ukv[:].rearrange("p k h t n -> p k (h t n)"), a["w_ukv"].rearrange("(k p) n -> p k n", p=P)).then_inc(aw_in[4], 16)
            for i in range(NT):
                sp.wait_ge(m.x, i + 1)
                sp.dma_start(x_mid[i * P:(i + 1) * P, :], xr[:, i, :]).then_inc(mid_out, 16)
            sp.wait_ge(q_ps, 2 * NH)
            sp.dma_start(w_o[:], a["w_o"][0].rearrange("(h p) n -> p h n", p=P)).then_inc(aw_in[5], 16)
            m = layers[1]
            sp.wait_ge(mid_out, 16 * NT)
            sp.wait_ge(a_xn, NT)
            for n, i in enumerate(WO_ORDER):
                if n == 4:
                    sp.wait_ge(o_ps, len(UNITS))
                sp.dma_start(xr[:, i, :], x_mid[i * P:(i + 1) * P, :]).then_inc(mid_in[n // 4], 16)
            load_first(m)
            load_experts(m)
            sp.wait_ge(m.all_out, m.turn)
            sp.dma_start(final_row[:], a["final_g"].partition_broadcast(P)).then_inc(misc_in, 16)
            dst = out[0].rearrange("(t p) d -> t p d", p=P)
            for i in range(NT):
                sp.wait_ge(f_ok, i + 1)
                sp.dma_start(dst[i], fin[i % 2][:]).then_inc(out_done[i % 2], 16)
            for u in range(2):
                sp.wait_ge(out_done[u], 16 * NT // 2)

        DVE_TAPS = 2 * (TAPS - SIDE_TAPS)

        @block.gpsimd
        def _(pool):
            own = Count(pool, pool_own)
            for t, v in ((ident, 0.0), (before, 1.0), (ones, 1.0), (causal, 0.0), (neghalf, -0.5)):
                own.chain(nc.gpsimd.memset(t[:], v))
            nc.gpsimd.affine_select(out=ident[:], in_=ident[:], compare_op=ALU.not_equal, fill=1.0, base=0,
                                    pattern=[[-1, P]], channel_multiplier=1).then_inc(consts_ok, 1)
            nc.gpsimd.affine_select(out=before[:], in_=before[:], compare_op=ALU.is_gt, fill=0.0, base=0,
                                    pattern=[[1, P]], channel_multiplier=-1).then_inc(consts_ok, 1)
            nc.gpsimd.affine_select(out=causal[:], in_=causal[:], compare_op=ALU.is_ge, fill=NEG, base=0,
                                    pattern=[[-1, P]], channel_multiplier=1).then_inc(consts_ok, 1)
            own.chain(nc.gpsimd.memset(zero[:], 0.0))

            def root(dst, src, scale, done):
                own.chain(nc.gpsimd.tensor_scalar(dst, src, scale, EPS, ALU.mult, ALU.add))
                nc.gpsimd.tensor_tensor(dst, dst, neghalf[:, 0:dst.shape[1]], ALU.pow).then_inc(done, 1)

            pool.wait_ge(ssq_ok, NT)
            root(rstd[:], ssq[:], 1.0 / D, rstd_ok)
            def split_w_in(c, u):
                pool.wait_ge(win_hi, c + 1)
                nc.gpsimd.tensor_tensor(w_in_l[:], w_in[u][:], w_in_h[:].bitcast(F32), ALU.subtract).then_inc(win_lo, 1)

            def clear(c):
                pool.dma_start(sorted_rows.rearrange("a b -> (a b)").rearrange("(c p r n) -> p c r n", c=KD, p=P, n=ZERO_N)[:, bass.ds(c, 1)]
                               .rearrange("p c r n -> p (c r) n"), zero[:].unsqueeze(1).to_broadcast([P, 8, ZERO_N])).then_inc(zeroed, 16)

            def side_taps(c, u):
                for n in range(1, SIDE_TAPS):
                    pool.wait_ge(side_ok, c * SIDE_TAPS + (n + 1))
                    if n > 1:
                        pool.wait_ge(side_used, c * (SIDE_TAPS - 1) + (n - 1))
                    nc.gpsimd.tensor_tensor(scratch[:], scratch[:], gate_row[:, n % 2, :], ALU.add).then_inc(side_used, 1)
                pool.wait_ge(side_used, c * (SIDE_TAPS - 1) + (SIDE_TAPS - 1))
                pool.wait_ge(tap_done, c * DVE_TAPS + DVE_TAPS)
                nc.gpsimd.tensor_tensor(acc[u][:], acc[u][:], scratch[:], ALU.add).then_inc(conv_sum, 1)

            nc.gpsimd.memset(sm[:, 46:47], 0.0).then_inc(conv_sum, 1)
            split_w_in(0, 0)
            split_w_in(1, 1)
            with pool.Fori(0, KD // 2 - 1) as j:
                for u in range(2):
                    side_taps(2 * j + u, u)
                    split_w_in(2 * j + (u + 2), u)
                    clear(2 * j + u)
            side_taps(KD - 2, 0)
            clear(KD - 2)
            clear(KD - 1)
            side_taps(KD - 1, 1)
            pool.wait_ge(ln_ok, NT)
            root(rstd[:], mv[:, :, 1], 1.0, ln_rstd)

            def scatter(m):
                pool.wait_ge(m.plan, m.turn)
                pool.wait_ge(zeroed, 16 * KD)
                for i in range(NT):
                    for d in (d_lo, d_hi):
                        pool.indirect_dma_start(sorted_rows, bass.IndirectOffsetOnAxis(ap=d[:, i:i + 1], axis=0), h_rows[:, i, :],
                                                None).then_inc(m.scattered, 16)

            mod_src = a["ada_w"][1].rearrange("(k p) n -> p k n", p=P)

            def products(x, steps):
                nc.gpsimd.tensor_tensor(x[:], x[:], c_col[:].unsqueeze(2).to_broadcast([P, KD, ADA_N]), ALU.mult).then_inc(part_step, 1)
                h, n = KD // 2, 1
                while h:
                    pool.wait_ge(part_step, steps + n)
                    nc.gpsimd.tensor_tensor(x[:, 0:h, :], x[:, 0:h, :], x[:, h:2 * h, :], ALU.add).then_inc(part_step, 1)
                    h, n = h // 2, n + 1

            STEPS = 4

            def load_early(n):
                pool.dma_start(ada_x0[n % 2][:], mod_src[:, :, n * ADA_N:(n + 1) * ADA_N]).then_inc(part_w, 16)

            def early(n):
                pool.wait_ge(part_w, 16 * n + 16)
                products(ada_x0[n % 2], STEPS * n)
                if n:
                    pool.wait_ge(part_out, 16 * n)
                if n + 1 < ADA_EARLY:
                    load_early(n + 1)
                pool.wait_ge(part_step, STEPS * (n + 1))
                pool.dma_start(ada_parts[:, n * ADA_N:(n + 1) * ADA_N], ada_x0[n % 2][:, 0, :]).then_inc(part_out, 16)

            def modulation():
                with pool.Fori(0, ADA_CHUNKS - ADA_EARLY) as g:
                    cols_g = bass.ds(g * ADA_N + ADA_EARLY * ADA_N, ADA_N)
                    steps = g * (STEPS + 2) + STEPS * ADA_EARLY
                    pool.dma_start(ada_x[:], mod_src[:, :, cols_g]).then_inc(part_w, 16)
                    pool.wait_ge(part_w, g * 16 + 16 * (ADA_EARLY + 1))
                    products(ada_x, steps)
                    pool.wait_ge(part_step, steps + STEPS)
                    nc.gpsimd.tensor_tensor(pool_mark[:], ident[:, 0:1], ident[:, 0:1], ALU.add).then_inc(part_step, 1)
                    pool.dma_start(ada_parts[:, cols_g], ada_x[:, 0, :]).then_inc(part_out, 16)
                    pool.wait_ge(part_step, steps + (STEPS + 1))
                    pool.wait_ge(part_out, g * 16 + 16 * (ADA_EARLY + 1))
                    nc.gpsimd.tensor_tensor(pool_mark[:], ident[:, 0:1], ident[:, 0:1], ALU.add).then_inc(part_step, 1)

            def roots(m):
                for n, i in enumerate(TILE_ORDER[m.l]):
                    pool.wait_ge(ssq_ok, (1 + 2 * m.l) * NT + n + 1)
                    root(rstd[:, i:i + 1], ssq[:, i:i + 1], 1.0 / D, rstd_ok)
                    if m.l == 0 and n < ADA_EARLY:
                        early(n)

            def gather(m, i):
                for n, d in enumerate((g_lo, g_hi)):
                    buf = 2 * (i % m.depth) + n
                    if i >= m.depth:
                        pool.wait_ge(m.x, m.n_x + i - m.depth + 1)
                    pool.indirect_dma_start(m.bufs[buf], None, sorted_rows, bass.IndirectOffsetOnAxis(ap=d[:, i:i + 1], axis=0)
                                            ).then_inc(rows_got[i % 4 if m.l else buf], 16)

            def last_roots(base, i):
                pool.wait_ge(ssq_ok, base + i + 1)
                root(rstd[:, i:i + 1], ssq[:, i:i + 1], 1.0 / D, rstd_ok)

            load_early(0)
            roots(layers[0])
            scatter(layers[0])
            modulation()
            pool.wait_ge(layers[0].all_out, 1)
            def q_roots(i):
                pool.wait_ge(a_ss, i + 1)
                own.chain(nc.gpsimd.tensor_scalar(sm[:, 16:17], sm[:, 0:1], 1.0 / KVR, EPS, ALU.mult, ALU.add))
                own.chain(nc.gpsimd.tensor_scalar(sm[:, 17:18], sm[:, 1:2], 1.0 / QR, EPS, ALU.mult, ALU.add))
                nc.gpsimd.tensor_tensor(sm[:, 18:20], sm[:, 16:18], neghalf[:, 0:2], ALU.pow).then_inc(a_r, 1)

            for i in range(NT + 3):
                if i < NT:
                    gather(layers[0], i)
                if 1 <= i <= NT:
                    last_roots(2 * NT, i - 1)
                if i >= 3:
                    q_roots(i - 3)
            roots(layers[1])
            scatter(layers[1])
            pool.wait_ge(layers[1].all_out, 2)
            for i in range(4):
                gather(layers[1], i)
            for i in range(NT):
                last_roots(4 * NT, i)
                if i + 4 < NT:
                    gather(layers[1], i + 4)

        @block.scalar
        def _(act_e):
            act_e.wait_ge(vec_ok, 1)
            nc.scalar.activation(c_col[:], col("c", 0, KD), ACT.Silu).then_inc(c_ok, 1)

            squared = Count(act_e, ssq_ok)

            def squares(i):
                if squared.n:
                    act_e.wait_ge(ssq_ok, squared.n)
                squared.n += 1
                nc.scalar.activation(scratch[:], xr[:, i, :], ACT.Square, accum_out=ssq[:, i:i + 1]).then_inc(ssq_ok, 1)

            for i in range(NT):
                act_e.wait_ge(x_in[i // 4], 64)
                squares(i)
            for b in range(ADA_FIRST // 2):
                act_e.wait_ge(ada_used, 2 * b + 2)
                nc.scalar.activation(ada_row[0:1, b * HALF:(b + 1) * HALF], ps[0:1, b, :], ACT.Copy).then_inc(ada_ev, 1)
            act_e.wait_ge(ada_ev, ADA_FIRST // 2)
            act_e.dma_start(ada_out[:, 0:ADA_FIRST * ADA_N], ada_row[0:1, :]).then_inc(ada_saved, 16)

            def ada_back_rows(a0, a1):
                act_e.dma_start(mod_rows[0:a1 - a0, :], ada_out.rearrange("a (r n) -> (a r) n", n=P)[a0:a1, :]).then_inc(ada_back, 16)

            act_e.wait_ge(ada_saved, 16)
            ada_back_rows(0, 2 * KD)
            def split_w_in(c, u):
                act_e.wait_ge(win_in[u], (c - u) * 16 + 32)
                nc.scalar.activation(w_in_h[:], w_in[u][:], ACT.Copy).then_inc(win_hi, 1)

            split_w_in(0, 0)
            for n in range(2 * KD):
                g, k = divmod(n, KD)
                act_e.wait_ge(in_T, n + 1)
                act_e.wait_ge(mod_first, 1)
                nc.scalar.activation(hT_h[:, k, g * HALF:(g + 1) * HALF], ps[:, n % 4, :], ACT.Identity, bias=mod(0, 0, k),
                                     scale=gainc[:, 0, k:k + 1]).then_inc(hT_ok, 1)
            act_e.wait_ge(ang_ok, 1)
            nc.scalar.activation(cosr[:], angle[1][:], ACT.Sin).then_inc(trig_ok, 1)
            nc.scalar.activation(sinr[:], angle[0][:], ACT.Sin).then_inc(trig_ok, 1)

            def gates(c):
                act_e.wait_ge(uv_ready, 2 * c + 2)
                for half in range(2):
                    nc.scalar.activation(sig[:, half, :], ps[:, 2 * half + 1, :], ACT.Sigmoid,
                                         bias=cols[:, bass.ds(c + (COL["conv_b_in"] + KD), 1)]).then_inc(sig_ok, 1)

            def ada_rows(c):
                act_e.wait_ge(ada_saved, c * 16 + 16)
                for n in range(ADA_PER_C):
                    act_e.wait_ge(ada_used, c * ADA_PER_C + (ADA_FIRST + n + 1))
                    nc.scalar.activation(ada_row[0:1, n * ADA_N:(n + 1) * ADA_N], ps[0:1, 6 + n % 2, 0:ADA_N], ACT.Copy).then_inc(ada_ev, 1)
                act_e.wait_ge(ada_ev, c * ADA_PER_C + (ADA_FIRST // 2 + ADA_PER_C))
                act_e.dma_start(ada_out[:, bass.ds(c * (ADA_PER_C * ADA_N) + ADA_FIRST * ADA_N, ADA_PER_C * ADA_N)],
                                ada_row[0:1, 0:ADA_PER_C * ADA_N]).then_inc(ada_saved, 16)

            def conv_out(c):
                for half in range(2):
                    act_e.wait_ge(conv_T, 2 * c + half + 1)
                    nc.scalar.activation(v_tok[:, 4 * half:4 * half + 4, bass.ds(c * P, P)],
                                         ps[:, 4 + half, :].rearrange("p (t n) -> p t n", n=P), ACT.Copy).then_inc(conv_ev, 1)

            def side_taps(c):
                act_e.wait_ge(uv_free, 2 * c + 4)
                act_e.wait_ge(conv_sum, c + 1)
                for n in range(SIDE_TAPS):
                    w = cols[:, bass.ds(c + (COL_DW + n * KD), 1)]
                    if n == 0:
                        nc.scalar.activation(scratch[:], glu[:, 0:S], ACT.Identity, bias=cols[:, bass.ds(c + COL["conv_b_dw"], 1)],
                                             scale=w).then_inc(side_ok, 1)
                    else:
                        if n > 2:
                            act_e.wait_ge(side_used, c * (SIDE_TAPS - 1) + (n - 2))
                        nc.scalar.activation(gate_row[:, n % 2, :], glu[:, n:n + S], ACT.Copy, scale=w).then_inc(side_ok, 1)

            gates(0)
            split_w_in(1, 1)
            ada_rows(0)
            side_taps(0)
            with act_e.Fori(0, KD // 2 - 1) as j:
                for u in range(2):
                    act_e.wait_ge(uv_ready, 4 * j + (2 * u + 4))
                    split_w_in(2 * j + (u + 2), u)
                    gates(2 * j + (u + 1))
                    ada_rows(2 * j + (u + 1))
                    conv_out(2 * j + u)
                    side_taps(2 * j + (u + 1))
            gates(KD - 1)
            side_taps(KD - 1)
            ada_rows(KD - 1)
            act_e.wait_ge(ada_saved, 16 + 16 * KD)
            ada_back_rows(2 * KD, 6 * KD)
            conv_out(KD - 2)
            conv_out(KD - 1)

            def gate_rows(l, rs):
                for r in rs:
                    act_e.wait_ge(row_ps, 4 * l + r + 1)
                    dst = gate_row if r < 2 else mod_row
                    nc.scalar.activation(dst[:, r % 2, :], banks(4 + 2 * (r % 2)), ACT.Copy).then_inc(row_ok, 1)

            gate_rows(0, range(4))

            def route(m, n):
                i = TILE_ORDER[m.l]
                if 1 <= n <= NT:
                    act_e.wait_ge((mixed, m_ev)[m.l], 2 * n)
                    squares(i[n - 1])
                if 2 <= n <= NT + 1:
                    act_e.wait_ge(m.T, m.n_x + n - 1)
                    if n >= 4:
                        act_e.wait_ge(m.logit, m.n_x + n - 3)
                    nc.scalar.activation(h2T[n % 2][:].rearrange("p k n -> p (k n)"), banks(2), ACT.Copy).then_inc(m.h2T, 1)

            for n in range(-1, NT + 2):
                if 0 <= n + 1 < NT:
                    act_e.wait_ge(vn_T, n + 2)
                    if n >= 1:
                        act_e.wait_ge(mix_ok, 2 * n)
                    for k in range(KD):
                        nc.scalar.activation(vT[(n + 1) % 2][:, k, :], banks(0)[:, k * P:(k + 1) * P], ACT.Silu,
                                             bias=col("conv_ln_b", k), scale=col("conv_ln_g", k)).then_inc(vT_ok, 1)
                route(layers[0], n)

            def moe(m):
                act_e.wait_ge(m.logit, m.n_x + NT)
                nc.scalar.activation(rt[:, 0, :], ps[:, 6, 0:P], ACT.Sigmoid).then_inc(m.score, 1)

                def split_hi(n, n_in):
                    act_e.wait_ge(m.w_in[n], n_in)
                    for c in range(PIECES):
                        nc.scalar.activation(part_h[n][:, c, :], raw[n][:, c, :], ACT.Copy).then_inc(m.hi[n], 1)

                def load_rows(b):
                    act_e.dma_start(rows[:], sorted_rows[bass.ds(b * P + P, P), :]).then_inc(m.rows_in, 16)

                def rowsT():
                    nc.scalar.activation(rowsT_h[:].rearrange("p k n -> p (k n)"), banks(2), ACT.Copy).then_inc(m.rowsT_h, 1)

                def hidT():
                    nc.scalar.activation(hidT_h[:].rearrange("p k n -> p (k n)"), ps[:, 4, :], ACT.Copy).then_inc(m.hidT_h, 1)

                def store(b):
                    act_e.wait_ge(m.y, b + 1)
                    act_e.dma_start(sorted_rows[bass.ds(b * P, P), :], y_sb[:]).then_inc(m.y_out, 16)

                act_e.wait_ge(m.plan, m.turn)
                split_hi(0, m.n_in + 16)
                act_e.wait_ge(m.scattered, 16 * 2 * NT * m.turn)
                load_rows(0)
                split_hi(1, m.n_in + 16)
                act_e.wait_ge(m.rows_T, 1)
                rowsT()
                load_rows(1)
                split_hi(2, m.n_in + 16)

                def expert(e, has_next):
                    first = act_e.value_load(starts[0:1, bass.ds(e, 1)], min_val=0, max_val=MAX_BLOCKS)
                    end = act_e.value_load(starts[0:1, bass.ds(e + 1, 1)], min_val=1, max_val=MAX_BLOCKS)
                    with act_e.Fori(first, end) as b:
                        act_e.wait_ge(m.gate, b + 1)
                        nc.scalar.activation(act[:], ps[:, 0, :], ACT.Silu).then_inc(m.silu, 1)
                        act_e.wait_ge(m.hid_T, b + 1)
                        hidT()
                        store(b)
                        if has_next:
                            with act_e.If(b + 1 == end):
                                split_hi(0, e * 16 + (m.n_in + 32))
                        act_e.wait_ge(m.rows_T, b + 2)
                        rowsT()
                        load_rows(b + 2)
                        if has_next:
                            with act_e.If(b + 1 == end):
                                split_hi(1, e * 16 + (m.n_in + 32))
                        with act_e.If(b == first):
                            act_e.wait_ge(m.down, b + 1)
                            split_hi(2, e * 16 + (m.n_in + 16))

                with act_e.Fori(0, NE - 1) as e:
                    expert(e, True)
                expert(NE - 1, False)
                total = act_e.value_load(starts[0:1, NE:NE + 1], min_val=NE, max_val=MAX_BLOCKS)
                act_e.wait_ge(m.hid_T, total + 1)
                hidT()
                store(total)
                store(total + 1)
                act_e.wait_ge(m.y_out, 16 * total + 32)
                act_e.wait_ge(m.rows_in, 16 * total + 32)
                nc.scalar.activation(sm[:, 40:41], sm[:, 40:41], ACT.Copy).then_inc(m.all_out, 1)

            def last_squares(m, i):
                act_e.wait_ge(m.x, m.n_x + i + 1)
                squares(i)

            moe(layers[0])

            def fold(name, k, dst):
                nc.scalar.activation(dst, dst, ACT.Copy, scale=col(name, k)).then_inc(folded, 1)

            def copy_xnT(i):
                act_e.wait_ge(a_T1, i + 1)
                if i >= 2:
                    act_e.wait_ge(a_M, i - 1)
                nc.scalar.activation(xnT[i % 2][:].rearrange("p k n -> p (k n)"), banks(0), ACT.Copy)
                for k in range(KD):
                    last = nc.scalar.activation(qinT[i % 2][:, k, :], banks(0)[:, k * P:(k + 1) * P], ACT.Identity, bias=mod(1, 0, k),
                                                scale=gainc[:, 2, k:k + 1])
                last.then_inc(a_xnT, 1)

            def latent_squares(i):
                act_e.wait_ge(a_M, i + 1)
                if i >= 1:
                    act_e.wait_ge(a_nrm, i)
                act_e.wait_ge(ssq_ok, squared.n)
                nc.scalar.activation(scratch[:, 0:KVR], ps[:, 2, 0:KVR], ACT.Square, accum_out=sm[:, 0:1])
                nc.scalar.activation(scratch[:, KVR:KVR + QR], ps[:, 3, 0:QR], ACT.Square, accum_out=sm[:, 1:2]).then_inc(a_ss, 1)

            def copy_latT(i):
                act_e.wait_ge(a_T2, i + 1)
                tok = slice(i * P, (i + 1) * P)
                nc.scalar.activation(latT[:, :, tok], ps[:, 4, 0:KVR].rearrange("p (k n) -> p k n", n=P), ACT.Copy).then_inc(a_ev2, 1)
                nc.scalar.activation(krT[:, tok], ps[:, 4, KVR:KVR + P], ACT.Copy).then_inc(a_ev2, 1)
                nc.scalar.activation(cqT[:, :, tok], ps[:, 5, 0:QR].rearrange("p (k n) -> p k n", n=P), ACT.Copy).then_inc(a_ev2, 1)

            def copy_qrT(i):
                act_e.wait_ge(a_T3, i + 1)
                nc.scalar.activation(qrT[:, :, i * P:(i + 1) * P], ps[:, 7, :].rearrange("p (k n) -> p k n", n=P),
                                     ACT.Copy).then_inc(a_ev3, 1)

            act_e.wait_ge(aw_in[0], 16)
            for k in range(KD):
                fold("kv_in_g", k, w_dkv[:, k, :])
            last_squares(layers[0], 0)
            last_squares(layers[0], 1)
            act_e.wait_ge(mod_ok, 2)
            copy_xnT(0)
            act_e.wait_ge(aw_in[2], 48)
            for k in range(QR // P):
                fold("q_norm_g", k, w_uqr[:, k].rearrange("p h n -> p (h n)"))
            for i in range(NT + 2):
                if i + 2 < NT:
                    if i >= 1:
                        act_e.wait_ge(a_ss, i)
                    last_squares(layers[0], i + 2)
                if i + 1 < NT:
                    copy_xnT(i + 1)
                if i < NT:
                    latent_squares(i)
                if 1 <= i <= NT:
                    copy_latT(i - 1)
                if i >= 2:
                    copy_qrT(i - 2)
            act_e.wait_ge(aw_in[4], 16)
            for k in range(KVR // P):
                fold("kv_norm_g", k, w_ukv[:, k].rearrange("p h t n -> p (h t n)"))
            act_e.wait_ge(aw_in[3], 48)
            for k in range(QR // P):
                fold("q_norm_g", k, w_uqn[:, k].rearrange("p h n -> p (h n)"))
            for n in range(2 * NH):
                act_e.wait_ge(k_ps, n + 1)
                h, half = divmod(n, 2)
                nc.scalar.activation(kT[:, h, half * HALF:(half + 1) * HALF], ps[:, n % 2, :], ACT.Copy).then_inc(k_ev, 1)
            gate_rows(1, range(2))
            for n in range(2 * NH):
                act_e.wait_ge(q_ps, n + 1)
                h, half = divmod(n, 2)
                nc.scalar.activation(qT[:, h, half * HALF:(half + 1) * HALF], ps[:, 4 + n % 2, :], ACT.Copy).then_inc(q_ev, 1)
            act_e.wait_ge(mid_out, 16 * NT)
            for u, (i, h) in enumerate(UNITS):
                n = (i + 1) * P
                act_e.wait_ge(nb_ok, u + 1)
                nc.scalar.activation(probs[u % 2][:, 0:n], banks(2 * (u % 2))[:, 0:n], ACT.Exp, bias=sm[:, 4 + u % 4:5 + u % 4],
                                     scale=ATTN_SCALE, accum_out=sm[:, 8 + u % 4:9 + u % 4]).then_inc(p_ok, 1)
                act_e.wait_ge(pT_ps, u + 1)
                n = min(n, HALF)
                nc.scalar.activation(probsT[u % 2][:, 0:n // P, :], ps[:, 4, 0:n].rearrange("p (k n) -> p k n", n=P),
                                     ACT.Copy).then_inc(pT_a, 1)
                if h == 1 and i > 0 or u == len(UNITS) - 1:
                    j = i - 1 if u < len(UNITS) - 1 else i
                    act_e.wait_ge(o_T, j + 1)
                    nc.scalar.activation(qT[:, 0:4, j * P:(j + 1) * P], ps[:, 6, :].rearrange("p (k n) -> p k n", n=P),
                                         ACT.Copy).then_inc(oT_a, 1)
            gate_rows(1, range(2, 4))
            for n in range(NT + 2):
                route(layers[1], n)
            moe(layers[1])
            for i in range(NT):
                last_squares(layers[1], i)

        @block.vector
        def _(dve):
            own = Count(dve, dve_own)
            ch = own.chain
            V = nc.vector

            dve.wait_ge(vec_in, 16 * (len(VEC_ROWS) + 4))
            ch(V.tensor_copy(pos_rows_f[0:NT, :], pos_rows[0:NT, :]))
            V.memset(glu[:, 0:PAD], 0.0).then_inc(uv_free, 2)
            V.memset(sm[:, 43:44], 0.0).then_inc(conv_ev, 2)
            dve.wait_ge(vec_T, 1)
            ch(V.tensor_copy(cols[:, 0:NVEC], ps[:, 7, 0:NVEC]))
            V.tensor_copy(cols[:, COL_ADA_B:NCOL], ps[:, 7, COL_ADA_B:NCOL]).then_inc(vec_ok, 1)
            dve.wait_ge(vec_ok, 1)

            def normalise(dst, i):
                return V.tensor_scalar(dst, xr[:, i, :], rstd[:, i:i + 1], None, ALU.mult)

            dve.wait_ge(rstd_ok, 1)
            for i in range(NT):
                normalise(v_tok[:, i, :], i).then_inc(xn_ok, 1)
            dve.wait_ge(misc_in, 48)
            for i in range(NT):
                ch(V.tensor_scalar(angle[0][:, i, :], invf[:], cols[:, COL_POS + i:COL_POS + i + 1], None, ALU.mult))
            ch(V.tensor_scalar(angle[1][:], angle[0][:], 1.0 / TWO_PI, ROUND, ALU.mult, ALU.add))
            ch(V.tensor_scalar(angle[1][:], angle[1][:], ROUND, None, ALU.subtract))
            for part in (C1, C2, C3):
                ch(V.scalar_tensor_tensor(angle[0][:], angle[1][:], -part, angle[0][:], ALU.mult, ALU.add))
            PI = float(np.nextafter(np.float32(np.pi), np.float32(0)))
            ch(V.tensor_scalar(angle[0][:], angle[0][:], PI, -PI, ALU.min, ALU.max))
            ch(V.tensor_scalar(angle[2][:], angle[0][:], -1.0, None, ALU.mult))
            ch(V.tensor_tensor(angle[1][:], angle[0][:], angle[2][:], ALU.max))
            V.tensor_scalar(angle[1][:], angle[1][:], -1.0, float(np.pi / 2), ALU.mult, ALU.add).then_inc(ang_ok, 1)
            dve.wait_ge(mod_T, 1)
            dve.wait_ge(xn_ok, NT)
            ch(V.tensor_tensor(modc[:, 0:16], ps[:, 6, 0:16], cols[:, COL_ADA_B:COL_ADA_B + 16], ALU.add))
            V.scalar_tensor_tensor(gainc[:, 0, :], mod(0, 1, 0, KD), 1.0, col("norm1_g", 0, KD), ALU.add, ALU.mult).then_inc(mod_first, 1)
            for n in range(2 * KD):
                g, k = divmod(n, KD)
                dve.wait_ge(hT_ok, n + 1)
                ch(V.tensor_scalar(sig[:, n % 2, :], ps[:, n % 4, :], gainc[:, 0, k:k + 1], mod(0, 0, k), ALU.mult, ALU.add))
                V.tensor_tensor(hT_l[:, k, g * HALF:(g + 1) * HALF], sig[:, n % 2, :],
                                hT_h[:, k, g * HALF:(g + 1) * HALF].bitcast(F32), ALU.subtract).then_inc(hT_lo, 1)

            def taps(c, u):
                for half in range(2):
                    dve.wait_ge(sig_ok, 2 * c + half + 1)
                    V.scalar_tensor_tensor(glu[:, PAD + half * HALF:PAD + (half + 1) * HALF], ps[:, 2 * half, :],
                                           cols[:, bass.ds(c + COL["conv_b_in"], 1)], sig[:, half, :], ALU.add,
                                           ALU.mult).then_inc(uv_free, 1)
                dve.wait_ge(uv_free, 2 * c + 4)
                for t in range(SIDE_TAPS, TAPS):
                    w = cols[:, bass.ds(c + (COL_DW + t * KD), 1)]
                    if t == TAPS - 1:
                        dve.wait_ge(side_ok, c * SIDE_TAPS + SIDE_TAPS)
                    for half in range(2):
                        src = glu[:, t + half * HALF:t + half * HALF + HALF]
                        dst = acc[u][:, half * HALF:(half + 1) * HALF]
                        if t == SIDE_TAPS:
                            V.tensor_scalar(dst, src, w, None, ALU.mult).then_inc(tap_done, 1)
                        else:
                            dve.wait_ge(tap_done, c * DVE_TAPS + (2 * (t - SIDE_TAPS) + half - 1))
                            V.scalar_tensor_tensor(dst, src, w, dst, ALU.mult, ALU.add).then_inc(tap_done, 1)
                dve.wait_ge(tap_done, c * DVE_TAPS + DVE_TAPS)

            with dve.Fori(0, KD // 2) as j:
                for u in range(2):
                    taps(2 * j + u, u)

            def stats(half):
                for i in range(NT):
                    dve.wait_ge(conv_ev, (half + 1) * KD + 2)
                    V.bn_stats(bst[:, 2 * i + half, :], v_tok[:, i, half * HALF:(half + 1) * HALF]).then_inc(dve_own, 1)
                    own.n += 1

            stats(0)
            dve.wait_ge(mod_T, 2)
            ch(V.tensor_tensor(modc[:, 16:48], ps[:, 7, 0:32], cols[:, COL_ADA_B + 16:COL_ADA_B + 48], ALU.add))

            def gain(l, r, name):
                return V.scalar_tensor_tensor(gainc[:, 2 * l + r, :], mod(l, 1 + 3 * r, 0, KD), 1.0, col(name, KD * l, KD), ALU.add, ALU.mult)

            ch(gain(0, 1, "norm2_g"))
            V.memset(sm[:], 0.0).then_inc(mod_ok, 1)

            def gate_rows(l, rs):
                for r in rs:
                    if l or r:
                        dve.wait_ge(row_ps, 4 * l + r)
                    for k in range(KD):
                        c = gainc[:, 2 * l + 1, k:k + 1] if r == 2 else mod(l, (2, 5, 4, 3)[r], k)
                        V.tensor_scalar(scratch[:, k * P:(k + 1) * P], ident[:], c, None, ALU.mult).then_inc(diag_ok, 1)

            stats(1)
            dve.wait_ge(dve_own, own.n)
            for i in range(NT):
                V.bn_aggr(mv[:, i, :], bst[:, 2 * i:2 * i + 2, :].rearrange("p a b -> p (a b)")).then_inc(ln_ok, 1)
            dve.wait_ge(ln_ok, NT)
            gate_rows(0, range(4))
            dve.wait_ge(ln_rstd, 1)

            def add_mixed(i, half, temp, ready, n, done):
                sl = slice(half * HALF, (half + 1) * HALF)
                dve.wait_ge(ready, n)
                ch(V.tensor_tensor(temp[:, sl], ps[:, 4 + half, :], gate_row[:, 0, sl], ALU.mult))
                V.tensor_tensor(xr[:, i, sl], xr[:, i, sl], temp[:, sl], ALU.add).then_inc(done, 1)

            def modulated(m, n):
                i = TILE_ORDER[m.l][n]
                dve.wait_ge(rstd_ok, (1, NT + 1 + NT)[m.l] + n + 1)
                ch(V.scalar_tensor_tensor(h_rows[:, i, :], xr[:, i, :], rstd[:, i:i + 1], mod_row[:, 0, :], ALU.mult, ALU.mult))
                V.tensor_tensor(h_rows[:, i, :], h_rows[:, i, :], mod_row[:, 1, :], ALU.add).then_inc(m.xn, 1)

            dve.wait_ge(row_ok, 4)
            for u in range(2):
                dve.wait_ge(x_in[u], 128)
            for n in range(-1, NT + 1):
                if n + 1 < NT:
                    i = n + 1
                    V.tensor_scalar(v_tok[:, i, :], v_tok[:, i, :], mv[:, i, 0:1], rstd[:, i:i + 1], ALU.subtract, ALU.mult).then_inc(vn_ok, 1)
                if n >= 1:
                    modulated(layers[0], n - 1)
                if 0 <= n < NT:
                    for half in range(2):
                        add_mixed(n, half, mix_t, mix_ok, 2 * n + half + 1, mixed)

            def moe(m):
                l = m.l
                dve.wait_ge(m.score, m.turn)
                s, sbias, rank, cmp_, mask, sM, work, pre, tot = (rt[:, n, :] for n in range(9))
                G = NT * NG
                per_j = rank.rearrange("p (j g) -> p j g", j=EPG)
                sb_g = sbias.rearrange("p (g j) -> p g j", j=EPG)
                ch(V.tensor_tensor(sbias.rearrange("p (t e) -> p t e", e=NE), s.rearrange("p (t e) -> p t e", e=NE),
                                   router_bias[:].unsqueeze(1).to_broadcast([P, NT, NE]), ALU.add))

                def ranks(n, rank, value, width):
                    for x in range(n):
                        ch(V.memset(rank[:, x, :], float(n - 1 - x)))
                    for x in range(n - 1):
                        m = n - 1 - x
                        c = cmp_[:, 0:m * width].rearrange("p (y w) -> p y w", w=width)
                        ch(V.tensor_tensor(c, value[:, x:x + 1, :].to_broadcast([P, m, width]), value[:, x + 1:, :], ALU.is_ge))
                        ch(V.tensor_tensor(rank[:, x + 1:, :], rank[:, x + 1:, :], c, ALU.add))
                        if m > 1:
                            won = work[:, 0:width]
                            ch(V.tensor_reduce(won, c.rearrange("p y w -> p w y"), AX_X, ALU.add))
                        else:
                            won = c[:, 0, :]
                        ch(V.tensor_tensor(rank[:, x, :], rank[:, x, :], won, ALU.subtract))

                ranks(EPG, per_j, sb_g.rearrange("p g j -> p j g"), G)
                ch(V.tensor_scalar(rank, rank, 1.5, None, ALU.is_lt))
                ch(V.tensor_tensor(work.rearrange("p (g j) -> p g j", j=EPG), sb_g, rank.rearrange("p (j g) -> p g j", j=EPG), ALU.mult))
                gs = rcol[:, 0:4, :].rearrange("p a b -> p (a b)")
                ch(V.tensor_reduce(gs, work.rearrange("p (g j) -> p g j", j=EPG), AX_X, ALU.add))
                gs_t = gs.rearrange("p (t g) -> p t g", g=NG)
                grank = rcol[:, 4:8, :]
                ranks(NG, grank, gs_t.rearrange("p t g -> p g t"), NT)
                ch(V.tensor_scalar(grank, grank, 0.5, None, ALU.is_lt))
                mask_j = mask.rearrange("p (t g j) -> p t g j", g=NG, j=EPG)
                for j in range(EPG):
                    ch(V.tensor_tensor(mask_j[:, :, :, j], per_j[:, j, :].rearrange("p (t g) -> p t g", g=NG),
                                       grank.rearrange("p g t -> p t g"), ALU.mult))
                V.tensor_tensor(sM, s, mask, ALU.mult).then_inc(m.mask, 1)
                dve.wait_ge(m.mask, m.turn)

                def by_expert(v):
                    return v.rearrange("p (t e) -> p t e", e=NE)

                def per_tile(v):
                    return v.unsqueeze(2).to_broadcast([P, NT, NE])

                wsum, rw, hi, lo = (rcol[:, n, :] for n in range(4))
                ch(V.tensor_reduce(wsum, by_expert(sM), AX_X, ALU.add))
                ch(V.reciprocal(rw, wsum))
                dve.wait_ge(m.rank, m.turn)
                ch(V.tensor_copy(pre, ps[:, 7, 0:P]))
                ch(V.tensor_copy(tot, ps[:, 7, P:2 * P]))
                so_far, t = [rt[:, 9, :], rt[:, 10, :]], 1
                ch(V.tensor_copy(so_far[0], tot))
                while t < NT:
                    ch(V.tensor_copy(so_far[1][:, 0:t * NE], so_far[0][:, 0:t * NE]))
                    ch(V.tensor_tensor(so_far[1][:, t * NE:], so_far[0][:, t * NE:], so_far[0][:, 0:(NT - t) * NE], ALU.add))
                    so_far, t = so_far[::-1], 2 * t
                ch(V.tensor_tensor(pre[:, NE:], pre[:, NE:], so_far[0][:, 0:(NT - 1) * NE], ALU.add))
                run = sm[:, 0:NE]
                ch(V.tensor_copy(run, so_far[0][:, (NT - 1) * NE:]))
                nblk, inc = sm[:, NE:2 * NE], [rt[:, 9, 0:NE], rt[:, 10, 0:NE]]
                ch(V.tensor_scalar(nblk, run, 1.0 / P, 0.5 - 0.25 / P, ALU.mult, ALU.add))
                ch(V.tensor_scalar(nblk, nblk, ROUND, None, ALU.add))
                ch(V.tensor_scalar(nblk, nblk, ROUND, 1.0, ALU.subtract, ALU.max))
                ch(V.tensor_copy(inc[0], nblk))
                cur, step = 0, 1
                while step < NE:
                    ch(V.tensor_copy(inc[1 - cur][:, 0:step], inc[cur][:, 0:step]))
                    ch(V.tensor_tensor(inc[1 - cur][:, step:], inc[cur][:, step:], inc[cur][:, 0:NE - step], ALU.add))
                    cur, step = 1 - cur, 2 * step
                first = rt[:, 11, 0:NE]
                ch(V.tensor_tensor(first, inc[cur], nblk, ALU.subtract))
                ch(V.tensor_copy(starts[:, 0:NE], first))
                ch(V.tensor_copy(starts[:, NE:NE + 1], inc[cur][:, NE - 1:NE]))
                ch(V.tensor_scalar(first, first, float(P), float(P + 1), ALU.mult, ALU.add))
                ch(V.tensor_tensor(by_expert(pre), by_expert(pre), first.unsqueeze(1).to_broadcast([P, NT, NE]), ALU.add))
                ch(V.tensor_tensor(pre, pre, mask, ALU.mult))
                ch(V.tensor_reduce(hi, by_expert(pre), AX_X, ALU.max))
                ch(V.tensor_reduce(lo, by_expert(pre), AX_X, ALU.add))
                ch(V.tensor_tensor(lo, lo, hi, ALU.subtract))
                for d, w, dest in ((hi, w_hi, d_hi), (lo, w_lo, d_lo)):
                    ch(V.tensor_tensor(by_expert(work), by_expert(pre), per_tile(d), ALU.is_equal))
                    ch(V.tensor_tensor(work, work, sM, ALU.mult))
                    ch(V.tensor_reduce(w[:], by_expert(work), AX_X, ALU.add))
                    ch(V.tensor_tensor(w[:], w[:], rw, ALU.mult))
                    ch(V.tensor_scalar(dest[:], d, -1.0, None, ALU.add))
                    ch(V.tensor_scalar((g_hi if w is w_hi else g_lo)[:], d, float(P - 1), None, ALU.add))
                V.memset(sm[:, 40:41], 0.0).then_inc(m.plan, 1)
                V.memset(y_sb[:], 0.0).then_inc(m.y, 1)
                V.memset(hid[:], 0.0).then_inc(m.hid, 1)

                def split_lo(n, count):
                    for c in range(PIECES):
                        dve.wait_ge(m.hi[n], count + (c + 1))
                        V.tensor_tensor(part_l[n][:, c, :], raw[n][:, c, :], part_h[n][:, c, :].bitcast(F32), ALU.subtract
                                        ).then_inc(m.lo[n], 1)

                def rowsT():
                    V.tensor_tensor(rowsT_l[:].rearrange("p k n -> p (k n)"), banks(2), rowsT_h[:].rearrange("p k n -> p (k n)").bitcast(F32),
                                    ALU.subtract).then_inc(m.rowsT_l, 1)

                def hidT():
                    V.tensor_tensor(hidT_l[:].rearrange("p k n -> p (k n)"), ps[:, 4, :], hidT_h[:].rearrange("p k n -> p (k n)").bitcast(F32),
                                    ALU.subtract).then_inc(m.hidT_l, 1)

                def output():
                    V.tensor_tensor(y_sb[:], banks(5), gate_row[:, 1, :], ALU.mult).then_inc(m.y, 1)

                split_lo(0, m.n_split)
                split_lo(1, m.n_split)
                dve.wait_ge(m.rowsT_h, 1)
                rowsT()
                split_lo(2, m.n_down)

                def expert(e, has_next):
                    first = dve.value_load(starts[0:1, bass.ds(e, 1)], min_val=0, max_val=MAX_BLOCKS)
                    end = dve.value_load(starts[0:1, bass.ds(e + 1, 1)], min_val=1, max_val=MAX_BLOCKS)
                    with dve.Fori(first, end) as b:
                        dve.wait_ge(m.hidT_h, b + 1)
                        hidT()
                        if has_next:
                            with dve.If(b + 1 == end):
                                split_lo(0, e * PIECES + (m.n_split + PIECES))
                        dve.wait_ge(m.silu, b + 1)
                        dve.wait_ge(m.up, b + 1)
                        V.tensor_tensor(hid[:], act[:], ps[:, 1, :], ALU.mult).then_inc(m.hid, 1)
                        dve.wait_ge(m.rowsT_h, b + 2)
                        rowsT()
                        if has_next:
                            with dve.If(b + 1 == end):
                                split_lo(1, e * PIECES + (m.n_split + PIECES))
                        dve.wait_ge(m.down, b + 1)
                        dve.wait_ge(m.y_out, b * 16 + 16)
                        output()
                        with dve.If(b == first):
                            split_lo(2, e * PIECES + (m.n_down + PIECES))

                with dve.Fori(0, NE - 1) as e:
                    expert(e, True)
                expert(NE - 1, False)
                total = dve.value_load(starts[0:1, NE:NE + 1], min_val=NE, max_val=MAX_BLOCKS)
                dve.wait_ge(m.hidT_h, total + 1)
                hidT()
                dve.wait_ge(m.down, total + 1)
                dve.wait_ge(m.y_out, total * 16 + 16)
                output()
                dve.wait_ge(x_back, 16 * NT * (l + 1))

            def combine(m, i):
                for n, w in enumerate((w_lo, w_hi)):
                    buf = 2 * (i % m.depth) + n
                    if m.l:
                        dve.wait_ge(rows_got[i % 4], 16 * NT // 2 + 32 * (i // 4 + 1))
                    else:
                        dve.wait_ge(rows_got[buf], 16 * (i // 2 + 1))
                    op = V.scalar_tensor_tensor(xr[:, i, :], m.bufs[buf], w[:, i:i + 1], xr[:, i, :], ALU.mult, ALU.add)
                    if n:
                        op.then_inc(m.x, 1)
                    else:
                        ch(op)

            moe(layers[0])

            def norm_tile(i):
                if i >= 2:
                    dve.wait_ge(a_T1, i - 1)
                dve.wait_ge(rstd_ok, 1 + NT + i + 1)
                normalise(xn_t[i % 2][:], i).then_inc(a_xn, 1)

            def rotate(dst1, dst2, x1, x2, cs, sn, t):
                ch(V.tensor_tensor(t[0], x1, cs, ALU.mult))
                ch(V.tensor_tensor(t[1], x2, sn, ALU.mult))
                ch(V.tensor_tensor(dst1, t[0], t[1], ALU.subtract))
                ch(V.tensor_tensor(t[0], x1, sn, ALU.mult))
                ch(V.tensor_tensor(t[1], x2, cs, ALU.mult))
                ch(V.tensor_tensor(dst2, t[0], t[1], ALU.add))

            def latents(i):
                u = i % 2
                if i >= 2:
                    dve.wait_ge(a_T2, i - 1)
                dve.wait_ge(a_r, i + 1)
                ch(V.tensor_scalar(lat[u][:, 0:2, :].rearrange("p a b -> p (a b)"), ps[:, 2, 0:KVR], sm[:, 18:19], None, ALU.mult))
                R2 = ROPE // 2
                twice = lat[u][:, 2, :].rearrange("p (c s n) -> p s c n", c=2, s=2)

                def both(v):
                    return v.unsqueeze(1).to_broadcast([P, 2, R2])

                t = [rope_t[:, n, 0:2, :] for n in range(2)]
                rotate(twice[:, 0], twice[:, 1], both(ps[:, 2, KVR:KVR + R2]), both(ps[:, 2, KVR + R2:KVR + ROPE]),
                       both(cosr[:, i, :]), both(sinr[:, i, :]), t)
                V.tensor_scalar(cqn[u][:].rearrange("p a b -> p (a b)"), ps[:, 3, 0:QR], sm[:, 19:20], None, ALU.mult).then_inc(a_nrm, 1)

            def rotate_q(i):
                u = i % 2
                R2 = ROPE // 2
                if i >= 2:
                    dve.wait_ge(a_T3, i - 1)
                dve.wait_ge(a_R, i + 1)
                x = ps[:, 6, :].rearrange("p (h n) -> p h n", n=ROPE)

                def heads(v):
                    return v.unsqueeze(1).to_broadcast([P, NH, R2])

                rotate(qro[u][:, :, 0:R2], qro[u][:, :, R2:], x[:, :, 0:R2], x[:, :, R2:], heads(cosr[:, i, :]), heads(sinr[:, i, :]),
                       [rope_t[:, 2 + n] for n in range(2)])
                V.memset(sm[:, 42:43], 0.0).then_inc(a_qr, 1)

            dve.wait_ge(trig_ok, 2)
            combine(layers[0], 0)
            combine(layers[0], 1)
            norm_tile(0)
            dve.wait_ge(mod_T, 3)
            ch(V.tensor_tensor(modc[:, 48:64], ps[:, 6, 0:16], cols[:, COL_ADA_B + 48:COL_ADA_B + 64], ALU.add))
            gain(1, 0, "norm1_g").then_inc(mod_ok, 1)
            combine(layers[0], 2)
            norm_tile(1)
            dve.wait_ge(mod_T, 4)
            ch(V.tensor_tensor(modc[:, 64:96], ps[:, 7, 0:32], cols[:, COL_ADA_B + 64:COL_ADA_B + 96], ALU.add))
            ch(gain(1, 1, "norm2_g"))
            for i in range(NT + 1):
                if i + 3 < NT:
                    combine(layers[0], i + 3)
                if i + 2 < NT:
                    norm_tile(i + 2)
                if i < NT:
                    latents(i)
                if i >= 1:
                    rotate_q(i - 1)
            gate_rows(1, range(2))
            for n in range(2 * NT):
                i, half = divmod(n, 2)
                dve.wait_ge(v_ps, n + 1)
                V.tensor_copy(v_all[:, i, 4 * half:4 * half + 4, :].rearrange("p h n -> p (h n)"), ps[:, 2 + n % 2, :]).then_inc(v_ev, 1)

            def maxima(u):
                i, h = UNITS[u]
                n = (i + 1) * P
                s = banks(2 * (u % 2))
                dve.wait_ge(s_ok, u + 1)
                ch(V.tensor_tensor(s[:, i * P:n], s[:, i * P:n], causal[:], ALU.add))
                ch(V.tensor_reduce(sm[:, 12 + u % 2:13 + u % 2], s[:, 0:n], AX_X, ALU.max))
                V.tensor_scalar(sm[:, 4 + u % 4:5 + u % 4], sm[:, 12 + u % 2:13 + u % 2], -ATTN_SCALE, None, ALU.mult).then_inc(nb_ok, 1)

            def outputs(u):
                i, h = UNITS[u]
                dve.wait_ge(p_ok, u + 1)
                ch(V.reciprocal(sm[:, 20 + u % 2:21 + u % 2], sm[:, 8 + u % 4:9 + u % 4]))
                dve.wait_ge(o_ps, u + 1)
                V.tensor_scalar(scratch[:, h * P:(h + 1) * P], ps[:, 6 + u % 2, 0:P], sm[:, 20 + u % 2:21 + u % 2], None, ALU.mult).then_inc(o_ok, 1)

            def out_T(i):
                dve.wait_ge(o_T, i + 1)
                V.tensor_copy(qT[:, 4:8, i * P:(i + 1) * P], ps[:, 7, :].rearrange("p (k n) -> p k n", n=P)).then_inc(oT_v, 1)

            for u in range(len(UNITS) + 2):
                if u < len(UNITS):
                    maxima(u)
                if 1 <= u <= len(UNITS):
                    i, h = UNITS[u - 1]
                    dve.wait_ge(pT_ps, u)
                    if i >= 4:
                        V.tensor_copy(probsT[(u - 1) % 2][:, 4:i + 1, :].rearrange("p a b -> p (a b)"),
                                      ps[:, 5, 0:(i - 3) * P]).then_inc(pT_v, 1)
                if u >= 2:
                    i, h = UNITS[u - 2]
                    if h == 0 and i:
                        out_T(i - 1)
                    outputs(u - 2)
            out_T(NT - 1)
            gate_rows(1, range(2, 4))
            dve.wait_ge(row_ok, 8)
            for n in range(NT + 1):
                if n:
                    modulated(layers[1], n - 1)
                if n < NT:
                    dve.wait_ge(mid_in[n // 4], 64)
                    for half in range(2):
                        add_mixed(WO_ORDER[n], half, mix_t2, m_ps, 2 * n + half + 1, m_ev)
            moe(layers[1])
            dve.wait_ge(misc_in, 64)
            for i in range(NT):
                if i == 0:
                    combine(layers[1], 0)
                if i + 1 < NT:
                    combine(layers[1], i + 1)
                dve.wait_ge(rstd_ok, 3 * NT + 1 + i + 1)
                if i >= 2:
                    dve.wait_ge(out_done[i % 2], 16 * (i // 2))
                V.scalar_tensor_tensor(fin[i % 2][:], xr[:, i, :], rstd[:, i:i + 1], final_row[:], ALU.mult, ALU.mult).then_inc(f_ok, 1)

        @block.tensor
        def _(pe):
            def T(dst, src, n=P):
                return nc.tensor.transpose(dst, src, ident[0:n, 0:n])

            def mm(dst, w, x, first, last):
                return nc.tensor.matmul(dst, w, x, start=first, stop=last)

            def three(dst, xh, xl, wh, wl, k, nk):
                mm(dst, xh, wh, k == 0, False)
                mm(dst, xh, wl, False, False)
                return mm(dst, xl, wh, False, k == nk - 1)

            pe.wait_ge(consts_ok, 3)
            pe.wait_ge(vec_in, 16 * (len(VEC_ROWS) + 4))
            T(ps[:, 7, 0:NVEC], vec_rows[0:NVEC, 0, :], NVEC)
            T(ps[:, 7, COL_ADA_B:COL_ADA_B + 96], vec_rows[0:96, 1, :], 96)
            for u in range(2):
                T(ps[:, 7, COL_DW + u * DW_ROWS:COL_DW + (u + 1) * DW_ROWS], vec_rows[0:DW_ROWS, 2 + u, :], DW_ROWS)
            pe.wait_ge(dve_own, 1)
            T(ps[:, 7, COL_POS:COL_POS + NT], pos_rows_f[0:NT, :], NT).then_inc(vec_T, 1)

            def ada(slot, n_in, dst):
                pe.wait_ge(ada_in[slot], n_in)
                for k in range(KD):
                    last = mm(dst, c_col[:, k:k + 1], ada_w[slot][:, k, :], k == 0, k == KD - 1)
                last.then_inc(ada_used, 1)

            pe.wait_ge(c_ok, 1)
            for g in range(ADA_FIRST):
                ada(ada_slot(g)[0], 16 * ada_slot(g)[1], ps[0:1, g // 2, (g % 2) * ADA_N:(g % 2 + 1) * ADA_N])
            pe.wait_ge(ada_ev, ADA_FIRST // 2)
            for n in range(2 * KD):
                g, k = divmod(n, KD)
                pe.wait_ge(xn_ok, 4 * (g + 1))
                if n == 4:
                    pe.wait_ge(ada_back, 16)
                    T(ps[:, 6, 0:2 * KD], mod_rows[0:2 * KD, :], 2 * KD).then_inc(mod_T, 1)
                if n >= 4:
                    pe.wait_ge(hT_lo, n - 3)
                for t in range(4):
                    last = T(ps[:, n % 4, t * P:(t + 1) * P], v_tok[:, 4 * g + t, k * P:(k + 1) * P])
                last.then_inc(in_T, 1)
            pe.wait_ge(hT_lo, 2 * KD)

            def conv_in(c, u):
                pe.wait_ge(win_lo, c + 1)
                for half in range(2):
                    pe.wait_ge(uv_free, 2 * c + half + 1)
                    for g in range(2):
                        for k in range(KD):
                            sl = slice(half * HALF, (half + 1) * HALF)
                            last = three(ps[:, 2 * half + g, :], w_in_h[:, k, g, :], w_in_l[:, k, g, :], hT_h[:, k, sl], hT_l[:, k, sl], k, KD)
                    last.then_inc(uv_ready, 1)
                for n in range(ADA_PER_C):
                    g = ADA_FIRST + n
                    pe.wait_ge(ada_ev, c * ADA_PER_C + (ADA_FIRST // 2 + max(n - 1, 0)))
                    slot, count = ada_slot(g)
                    ada(slot, c * (16 * ada_per_c(slot)) + 16 * count, ps[0:1, 6 + n % 2, 0:ADA_N])

            def conv_T_tile(c, u):
                pe.wait_ge(conv_sum, c + 2)
                pe.wait_ge(conv_ev, 2 * c + 2)
                for half in range(2):
                    for t in range(4):
                        last = T(ps[:, 4 + half, t * P:(t + 1) * P], acc[u][:, (4 * half + t) * P:(4 * half + t + 1) * P])
                    last.then_inc(conv_T, 1)

            conv_in(0, 0)
            with pe.Fori(0, KD // 2 - 1) as j:
                for u in range(2):
                    conv_in(2 * j + (u + 1), 1 - u)
                    conv_T_tile(2 * j + u, u)
            conv_in(KD - 1, 1)
            conv_T_tile(KD - 2, 0)
            conv_T_tile(KD - 1, 1)

            def gate_rows(l, rs):
                for r in rs:
                    if r >= 2:
                        pe.wait_ge(row_ok, 4 * l + r - 1)
                    for k in range(KD):
                        pe.wait_ge(diag_ok, KD * (4 * l + r) + k + 1)
                        last = mm(ps[:, 4 + 2 * (r % 2) + k // 4, (k % 4) * P:(k % 4 + 1) * P], ones[:], scratch[:, k * P:(k + 1) * P], True, True)
                    last.then_inc(row_ps, 1)

            pe.wait_ge(ada_back, 32)
            T(ps[:, 7, 0:4 * KD], mod_rows[0:4 * KD, :], 4 * KD).then_inc(mod_T, 1)
            pe.wait_ge(mod_ok, 1)
            pe.wait_ge(conv_ev, 2 * KD + 2)
            gate_rows(0, range(4))
            pe.wait_ge(row_ok, 4)
            pe.wait_ge(wout_in, 16)

            def vn_tile(i):
                pe.wait_ge(vn_ok, i + 1)
                if i:
                    pe.wait_ge(vT_ok, KD * i)
                for k in range(KD):
                    last = T(banks(0)[:, k * P:(k + 1) * P], v_tok[:, i, k * P:(k + 1) * P])
                last.then_inc(vn_T, 1)

            def route(m, n):
                if 1 <= n <= NT:
                    i = TILE_ORDER[m.l][n - 1]
                    pe.wait_ge(m.xn, m.n_x + n)
                    if n >= 2:
                        pe.wait_ge(m.h2T, m.n_x + n - 1)
                    for k in range(KD):
                        last = T(banks(2)[:, k * P:(k + 1) * P], h_rows[:, i, k * P:(k + 1) * P])
                    last.then_inc(m.T, 1)
                if 2 <= n <= NT + 1:
                    i = TILE_ORDER[m.l][n - 2]
                    pe.wait_ge(m.h2T, m.n_x + n - 1)
                    for k in range(KD):
                        last = mm(ps[:, 6, i * NE:(i + 1) * NE], h2T[n % 2][:, k, :], router[:, k, :], k == 0, k == KD - 1)
                    last.then_inc(m.logit, 1)

            vn_tile(0)
            for n in range(NT + 2):
                if n + 1 < NT:
                    vn_tile(n + 1)
                if n < NT:
                    pe.wait_ge(vT_ok, KD * (n + 1))
                    for half in range(2):
                        if n:
                            pe.wait_ge(mixed, 2 * (n - 1) + half + 1)
                        for k in range(KD):
                            last = mm(ps[:, 4 + half, :], vT[n % 2][:, k, :], w_out[:, k, half * HALF:(half + 1) * HALF],
                                      k == 0, k == KD - 1)
                        last.then_inc(mix_ok, 1)
                route(layers[0], n)

            def moe(m):
                pe.wait_ge(m.mask, m.turn)
                mm(ps[:, 7, 0:P], before[:], rt[:, 4, :], True, True)
                mm(ps[:, 7, P:2 * P], ones[:], rt[:, 4, :], True, True).then_inc(m.rank, 1)

                def rows_T(b):
                    pe.wait_ge(m.rows_in, b * 16 + 16)
                    for k in range(KD):
                        last = T(banks(2)[:, k * P:(k + 1) * P], rows[:, k * P:(k + 1) * P])
                    last.then_inc(m.rows_T, 1)

                pe.wait_ge(m.plan, m.turn)
                rows_T(0)

                def wide(n, bank):
                    wh, wl = (v[n][:].rearrange("p c (k n) -> p (c k) n", n=DE) for v in (part_h, part_l))
                    for k in range(KD):
                        last = three(ps[:, bank, :], rowsT_h[:, k, :], rowsT_l[:, k, :], wh[:, k, :], wl[:, k, :], k, KD)
                    return last

                def hid_T():
                    for k in range(DE // P):
                        last = T(ps[:, 4, k * P:(k + 1) * P], hid[:, k * P:(k + 1) * P])
                    last.then_inc(m.hid_T, 1)

                def down():
                    for half in range(2):
                        sl = slice(half * HALF, (half + 1) * HALF)
                        for k in range(DE // P):
                            last = three(ps[:, 5 + half, :], hidT_h[:, k, :], hidT_l[:, k, :], part_h[2][:, k, sl], part_l[2][:, k, sl],
                                         k, DE // P)
                    last.then_inc(m.down, 1)

                with pe.Fori(0, NE) as e:
                    first = pe.value_load(starts[0:1, bass.ds(e, 1)], min_val=0, max_val=MAX_BLOCKS)
                    end = pe.value_load(starts[0:1, bass.ds(e + 1, 1)], min_val=1, max_val=MAX_BLOCKS)
                    with pe.Fori(first, end) as b:
                        pe.wait_ge(m.lo[0], e * PIECES + (m.n_split + PIECES))
                        pe.wait_ge(m.rowsT_l, b + 1)
                        wide(0, 0).then_inc(m.gate, 1)
                        pe.wait_ge(m.hid, b + 1)
                        hid_T()
                        pe.wait_ge(m.lo[1], e * PIECES + (m.n_split + PIECES))
                        wide(1, 1).then_inc(m.up, 1)
                        rows_T(b + 1)
                        pe.wait_ge(m.hidT_l, b + 1)
                        pe.wait_ge(m.lo[2], e * PIECES + (m.n_down + PIECES))
                        pe.wait_ge(m.y, b + 1)
                        down()
                total = pe.value_load(starts[0:1, NE:NE + 1], min_val=NE, max_val=MAX_BLOCKS)
                pe.wait_ge(m.hid, total + 1)
                hid_T()
                pe.wait_ge(m.hidT_l, total + 1)
                pe.wait_ge(m.y, total + 1)
                down()

            moe(layers[0])

            def sum_parts(bank, parts):
                for n, src in enumerate(parts):
                    last = mm(ps[:, bank, n:n + 1], src, ones[:, 0:1], True, True)
                last.then_inc(mod_T, 1)

            pe.wait_ge(part_in[0], 16)
            sum_parts(6, [ada_p[:, k * P:(k + 1) * P] for k in range(2 * KD)])

            def T1(i):
                pe.wait_ge(a_xn, i + 1)
                if i:
                    pe.wait_ge(a_xnT, i)
                for k in range(KD):
                    last = T(banks(0)[:, k * P:(k + 1) * P], xn_t[i % 2][:, k * P:(k + 1) * P])
                last.then_inc(a_T1, 1)

            def M(i):
                pe.wait_ge(a_xnT, i + 1)
                if i:
                    pe.wait_ge(a_nrm, i)
                for k in range(KD):
                    mm(ps[:, 2, 0:KVR + ROPE], xnT[i % 2][:, k, :], w_dkv[:, k, :], k == 0, k == KD - 1)
                for k in range(KD):
                    last = mm(ps[:, 3, 0:QR], qinT[i % 2][:, k, :], w_dq[:, k, :], k == 0, k == KD - 1)
                last.then_inc(a_M, 1)

            def T2(i):
                pe.wait_ge(a_nrm, i + 1)
                for k in range(3):
                    T(ps[:, 4, k * P:(k + 1) * P], lat[i % 2][:, k, :])
                for k in range(3):
                    last = T(ps[:, 5, k * P:(k + 1) * P], cqn[i % 2][:, k, :])
                last.then_inc(a_T2, 1)

            def rope_q(i):
                pe.wait_ge(a_ev2, 3 * (i + 1))
                if i:
                    pe.wait_ge(a_qr, i)
                for k in range(QR // P):
                    last = mm(ps[:, 6, :], cqT[:, k, i * P:(i + 1) * P], w_uqr[:, k].rearrange("p h n -> p (h n)"), k == 0, k == QR // P - 1)
                last.then_inc(a_R, 1)

            def T3(i):
                pe.wait_ge(a_qr, i + 1)
                if i:
                    pe.wait_ge(a_ev3, i)
                x = qro[i % 2][:].rearrange("p h n -> p (h n)")
                for k in range(NH // 2):
                    last = T(ps[:, 7, k * P:(k + 1) * P], x[:, k * P:(k + 1) * P])
                last.then_inc(a_T3, 1)

            T1(0)
            pe.wait_ge(part_in[1], 32)
            sum_parts(7, [ada_p[:, k * P:(k + 1) * P] for k in range(2 * KD, 5 * KD)] + [ada_p5[:, k * P:(k + 1) * P] for k in range(KD)])
            pe.wait_ge(folded, KD)
            pe.wait_ge(aw_in[1], 16)
            for i in range(NT + 2):
                if i + 1 < NT:
                    T1(i + 1)
                if i < NT:
                    M(i)
                if 1 <= i <= NT:
                    T2(i - 1)
                    if i == 1:
                        pe.wait_ge(folded, KD + QR // P)
                    rope_q(i - 1)
                if i >= 2:
                    T3(i - 2)
            pe.wait_ge(a_ev3, NT)
            pe.wait_ge(folded, KD + QR // P + KVR // P)
            for n in range(2 * NH):
                h, half = divmod(n, 2)
                if n >= 2:
                    pe.wait_ge(k_ev, n - 1)
                for k in range(KVR // P):
                    last = mm(ps[:, n % 2, :], w_ukv[:, k, h, 0, :], latT[:, k, half * HALF:(half + 1) * HALF], k == 0, k == KVR // P - 1)
                last.then_inc(k_ps, 1)
            gate_rows(1, range(2))
            for n in range(2 * NT):
                i, half = divmod(n, 2)
                if n >= 2:
                    pe.wait_ge(v_ev, n - 1)
                for k in range(KVR // P):
                    last = mm(ps[:, 2 + n % 2, :], latT[:, k, i * P:(i + 1) * P], w_ukv[:, k, 4 * half:4 * half + 4, 1, :], k == 0, k == KVR // P - 1)
                last.then_inc(v_ps, 1)
            pe.wait_ge(row_ok, 6)
            pe.wait_ge(folded, KD + 2 * (QR // P) + KVR // P)
            for n in range(2 * NH):
                h, half = divmod(n, 2)
                if n >= 2:
                    pe.wait_ge(q_ev, n - 1)
                for k in range(QR // P):
                    last = mm(ps[:, 4 + n % 2, :], w_uqn[:, k, h, :], cqT[:, k, half * HALF:(half + 1) * HALF], k == 0, k == QR // P - 1)
                last.then_inc(q_ps, 1)
            pe.wait_ge(k_ev, 2 * NH)
            pe.wait_ge(v_ev, 2 * NT)
            pe.wait_ge(q_ev, 2 * NH)

            def scores(u):
                i, h = UNITS[u]
                n = (i + 1) * P
                if u >= 2:
                    pe.wait_ge(p_ok, u - 1)
                half_p = slice(ROPE * (h % 2), ROPE * (h % 2) + ROPE)
                tok = slice(i * P, (i + 1) * P)
                for c in range(0, n, HALF):
                    w = min(HALF, n - c)
                    dst = ps[:, 2 * (u % 2) + c // HALF, 0:w]
                    mm(dst, qT[:, h, tok], kT[:, h, c:c + w], True, False)
                    last = mm(dst, qrT[half_p, h // 2, tok], krT[half_p, c:c + w], False, True)
                last.then_inc(s_ok, 1)

            def probs_T(u):
                i, h = UNITS[u]
                pe.wait_ge(p_ok, u + 1)
                if u:
                    pe.wait_ge(pT_a, u)
                    if UNITS[u - 1][0] >= 4:
                        pe.wait_ge(pT_v, u - 4 * NH)
                for j in range(i + 1):
                    last = T(ps[:, 4 + j // 4, (j % 4) * P:(j % 4 + 1) * P], probs[u % 2][:, j * P:(j + 1) * P])
                last.then_inc(pT_ps, 1)

            def out_T(i):
                pe.wait_ge(o_ok, NH * (i + 1))
                for k in range(NH):
                    last = T(ps[:, 6 + k // 4, (k % 4) * P:(k % 4 + 1) * P], scratch[:, k * P:(k + 1) * P])
                last.then_inc(o_T, 1)

            def output(u):
                i, h = UNITS[u]
                pe.wait_ge(pT_a, u + 1)
                if i >= 4:
                    pe.wait_ge(pT_v, u - 4 * NH + 1)
                if u >= 2:
                    pe.wait_ge(o_ok, u - 1)
                if h < 2 and i:
                    pe.wait_ge(oT_a, i)
                    pe.wait_ge(oT_v, i)
                for j in range(i + 1):
                    last = mm(ps[:, 6 + u % 2, 0:P], probsT[u % 2][:, j, :], v_all[:, j, h, :], j == 0, j == i)
                last.then_inc(o_ps, 1)

            scores(0)
            for u in range(len(UNITS) + 1):
                if u + 1 < len(UNITS):
                    scores(u + 1)
                if u < len(UNITS):
                    probs_T(u)
                if u:
                    i, h = UNITS[u - 1]
                    if h == 0 and i:
                        out_T(i - 1)
                    output(u - 1)
            out_T(NT - 1)
            pe.wait_ge(oT_a, NT)
            pe.wait_ge(oT_v, NT)
            pe.wait_ge(aw_in[5], 16)
            gate_rows(1, range(2, 4))
            pe.wait_ge(row_ok, 8)
            for n in range(NT + 2):
                if n < NT:
                    i = WO_ORDER[n]
                    for half in range(2):
                        if n:
                            pe.wait_ge(m_ev, 2 * (n - 1) + half + 1)
                        for h in range(NH):
                            last = mm(ps[:, 4 + half, :], qT[:, h, i * P:(i + 1) * P], w_o[:, h, half * HALF:(half + 1) * HALF],
                                      h == 0, h == NH - 1)
                        last.then_inc(m_ps, 1)
                route(layers[1], n)
            moe(layers[1])


class Count:

    def __init__(self, engine, own):
        self.engine, self.own, self.n = engine, own, 0

    def chain(self, instruction):
        self.n += 1
        instruction.then_inc(self.own, 1)
        self.engine.wait_ge(self.own, self.n)


INPUTS = ["x", "c", "positions", "ada_w", "ada_b", "norm1_g", "norm2_g", "conv_w_in", "conv_b_in", "conv_w_dw", "conv_b_dw",
          "conv_ln_g", "conv_ln_b", "conv_w_out", "kv_in_g", "w_dkv", "kv_norm_g", "w_ukv", "w_dq", "q_norm_g", "w_uq", "w_o",
          "router_w", "router_b", "exp_w_gate", "exp_w_up", "exp_w_down", "final_g"]


def kernel(**inputs):
    import concourse.bacc as bacc
    from concourse.bass_utils import run_bass_kernel_spmd

    nc = bacc.Bacc("TRN2", target_bir_lowering=False, num_devices=1)
    arrays = {f"in_{n}": np.ascontiguousarray(inputs[n]) for n in INPUTS}
    arrays["in_inv_freq"] = (np.float32(10000.0) ** (-np.arange(0, ROPE, 2, dtype=np.float32) / np.float32(ROPE))).astype(np.float32)
    aps = {n[3:]: nc.dram_tensor(n, v.shape, mybir.dt.from_np(v.dtype), kind="ExternalInput").ap() for n, v in arrays.items()}
    out = nc.dram_tensor("out", (1, S, D), F32, kind="ExternalOutput").ap()
    build_trunk(nc, aps, out)
    r = run_bass_kernel_spmd(nc, [arrays], core_ids=[0])
    return r.results[0]["out"]
```
